# Optimizing a Trainium2 kernel written in Bass

```python
import jax, jax.numpy as jnp
from jax import lax
import numpy as np

D_MODEL = 1024
BATCH = 1
SEQ = 2048
DEPTH = 1

D_MIX = D_MODEL
D_MLSTM = D_MIX // 2
D_CONV = D_MIX - D_MLSTM
N_MLSTM_HEADS = 4
HEAD_DIM = D_MLSTM // N_MLSTM_HEADS
CONV_WIDTH = 3
CHUNK = 128
N_EXPERTS = 16
N_GROUPS = 4
EXPERTS_PER_GROUP = N_EXPERTS // N_GROUPS
TOP_K = 2
D_FF_EXPERT = D_MODEL // 2
EXPERT_BLOCK = 128
LN_EPS = 1e-5
ALPHA = (2 * DEPTH) ** 0.25
BETA = (8 * DEPTH) ** -0.25

OFF_Q = 0
OFF_K = OFF_Q + D_MLSTM
OFF_V = OFF_K + D_MLSTM
OFF_O = OFF_V + D_MLSTM
OFF_I = OFF_O + D_MLSTM
OFF_F = OFF_I + N_MLSTM_HEADS
OFF_B = OFF_F + N_MLSTM_HEADS
OFF_C = OFF_B + D_CONV
OFF_X = OFF_C + D_CONV
P_IN = OFF_X + D_CONV

kernel_name = "hybrid_mlstm_shortconv_grouped_moe_deepnorm"

def layer_norm(x, g, b):
    xf = x.astype(jnp.float32)
    mu = xf.mean(-1, keepdims=True)
    var = jnp.square(xf - mu).mean(-1, keepdims=True)
    return ((xf - mu) * lax.rsqrt(var + LN_EPS) * g.astype(jnp.float32) + b.astype(jnp.float32)).astype(x.dtype)

def mlstm_cell(q, k, v, i_pre, f_pre):
    b, s, h, dh = q.shape
    nc = s // CHUNK
    f32 = jnp.float32

    def chunks(t):
        return t.astype(f32).reshape(b, nc, CHUNK, h, -1).transpose(0, 3, 1, 2, 4)

    q = chunks(q)
    k = chunks(k) * (dh ** -0.5)
    v = chunks(v)
    ig = chunks(i_pre[..., None])[..., 0]
    logf = jax.nn.log_sigmoid(chunks(f_pre[..., None])[..., 0])
    a = jnp.cumsum(logf, axis=-1)
    g = a[..., -1]

    w_end = g[..., None] - a + ig
    m_loc = w_end.max(-1)
    e_end = jnp.exp(w_end - m_loc[..., None])
    c_loc = jnp.einsum('bhcsk,bhcsv->bhckv', k * e_end[..., None], v)
    n_loc = jnp.einsum('bhcs,bhcsk->bhck', e_end, k)

    def step(carry, xs):
        c_prev, n_prev, m_prev = carry
        c_l, n_l, m_l, g_c = xs
        m_new = jnp.maximum(g_c + m_prev, m_l)
        s_prev = jnp.exp(g_c + m_prev - m_new)
        s_loc = jnp.exp(m_l - m_new)
        c_new = s_prev[..., None, None] * c_prev + s_loc[..., None, None] * c_l
        n_new = s_prev[..., None] * n_prev + s_loc[..., None] * n_l
        return (c_new, n_new, m_new), (c_prev, n_prev, m_prev)

    init = (jnp.zeros((b, h, dh, dh), f32), jnp.zeros((b, h, dh), f32), jnp.zeros((b, h), f32))
    xs = (jnp.moveaxis(c_loc, 2, 0), jnp.moveaxis(n_loc, 2, 0), jnp.moveaxis(m_loc, 2, 0), jnp.moveaxis(g, 2, 0))
    _, (c_st, n_st, m_st) = lax.scan(step, init, xs)
    c_st = jnp.moveaxis(c_st, 0, 2)
    n_st = jnp.moveaxis(n_st, 0, 2)
    m_st = jnp.moveaxis(m_st, 0, 2)

    causal = jnp.tril(jnp.ones((CHUNK, CHUNK), dtype=bool))
    log_d = jnp.where(causal, a[..., :, None] - a[..., None, :] + ig[..., None, :], -jnp.inf)
    log_inter = a + m_st[..., None]
    m_out = jnp.maximum(log_inter, log_d.max(-1))
    dmat = jnp.exp(log_d - m_out[..., None])
    s_qk = jnp.einsum('bhcjd,bhcsd->bhcjs', q, k) * dmat
    e_inter = jnp.exp(log_inter - m_out)
    num = jnp.einsum('bhcjs,bhcsv->bhcjv', s_qk, v) + e_inter[..., None] * jnp.einsum('bhcjk,bhckv->bhcjv', q, c_st)
    den = s_qk.sum(-1) + e_inter * jnp.einsum('bhcjk,bhck->bhcj', q, n_st)
    h_t = num / jnp.maximum(jnp.abs(den), jnp.exp(-m_out))[..., None]
    return h_t.transpose(0, 2, 3, 1, 4).reshape(b, s, h, dh)

def hybrid_mixer(x, w_in, b_in, conv_w, mh_g, w_out):
    b, s, _ = x.shape
    p = x @ w_in + b_in
    q = p[..., OFF_Q:OFF_K].reshape(b, s, N_MLSTM_HEADS, HEAD_DIM)
    k = p[..., OFF_K:OFF_V].reshape(b, s, N_MLSTM_HEADS, HEAD_DIM)
    v = p[..., OFF_V:OFF_O].reshape(b, s, N_MLSTM_HEADS, HEAD_DIM)
    o = p[..., OFF_O:OFF_I]
    i_pre = p[..., OFF_I:OFF_F]
    f_pre = p[..., OFF_F:OFF_B]
    h = mlstm_cell(q, k, v, i_pre, f_pre)
    mu = h.mean(-1, keepdims=True)
    var = jnp.square(h - mu).mean(-1, keepdims=True)
    h = (h - mu) * lax.rsqrt(var + LN_EPS) * mh_g.astype(jnp.float32).reshape(N_MLSTM_HEADS, HEAD_DIM)
    y_m = (jax.nn.sigmoid(o.astype(jnp.float32)) * h.reshape(b, s, D_MLSTM)).astype(x.dtype)

    gate_b = p[..., OFF_B:OFF_C]
    gate_c = p[..., OFF_C:OFF_X]
    xc = p[..., OFF_X:P_IN]
    u = gate_c * xc
    conv = lax.conv_general_dilated(u, conv_w[:, None, :].astype(u.dtype), window_strides=(1,),
                                    padding=[(CONV_WIDTH - 1, 0)], dimension_numbers=('NWC', 'WIO', 'NWC'),
                                    feature_group_count=D_CONV)
    y_c = gate_b * conv
    return jnp.concatenate([y_m, y_c], axis=-1) @ w_out

def grouped_moe(x, router_w, router_b, w_gate, w_up, w_down):
    b, s, d = x.shape
    n = b * s
    xf = x.reshape(n, d)
    probs = jax.nn.softmax((xf @ router_w).astype(jnp.float32) + router_b.astype(jnp.float32), axis=-1)
    pg = probs.reshape(n, N_GROUPS, EXPERTS_PER_GROUP)
    grp = jnp.argmax(lax.top_k(pg, TOP_K)[0].sum(-1), axis=-1)
    in_grp = jnp.take_along_axis(pg, grp[:, None, None], axis=1)[:, 0]
    top_p, top_local = lax.top_k(in_grp, TOP_K)
    expert_idx = grp[:, None] * EXPERTS_PER_GROUP + top_local
    gates = top_p / top_p.sum(-1, keepdims=True)

    flat_e = expert_idx.reshape(-1)
    order = jnp.argsort(flat_e)
    e_sorted = flat_e[order]
    tok_sorted = order // TOP_K
    gate_sorted = gates.reshape(-1)[order]
    counts = jnp.bincount(flat_e, length=N_EXPERTS)
    padded = (counts + EXPERT_BLOCK - 1) // EXPERT_BLOCK * EXPERT_BLOCK
    pad_end = jnp.cumsum(padded)
    pad_start = pad_end - padded
    start = jnp.cumsum(counts) - counts
    dest = pad_start[e_sorted] + (jnp.arange(n * TOP_K) - start[e_sorted])
    n_blocks = (n * TOP_K + EXPERT_BLOCK - 1) // EXPERT_BLOCK + N_EXPERTS
    buf = jnp.zeros((n_blocks * EXPERT_BLOCK, d), x.dtype).at[dest].set(xf[tok_sorted])
    block_expert = jnp.minimum(
        jnp.searchsorted(pad_end, jnp.arange(n_blocks) * EXPERT_BLOCK, side='right'), N_EXPERTS - 1)

    def expert_block(args):
        xb, e = args
        hdn = jax.nn.silu(xb @ w_gate[e]) * (xb @ w_up[e])
        return hdn @ w_down[e]

    y_buf = lax.map(expert_block, (buf.reshape(n_blocks, EXPERT_BLOCK, d), block_expert)).reshape(-1, d)
    y = y_buf[dest] * gate_sorted[:, None].astype(x.dtype)
    return jnp.zeros_like(xf).at[tok_sorted].add(y).reshape(b, s, d)

def setup_inputs(seed: int = 0) -> dict:
    key = jax.random.key(seed)
    ks = jax.random.split(key, 16)
    f32 = jnp.float32
    x = jax.random.normal(ks[0], (BATCH, SEQ, D_MODEL), f32)
    col_scale = jnp.ones((P_IN,), f32).at[OFF_V:OFF_O].set(BETA).at[OFF_X:P_IN].set(BETA)
    w_in = jax.random.normal(ks[1], (DEPTH, D_MODEL, P_IN), f32) * (D_MODEL ** -0.5) * col_scale
    b_in = (0.02 * jax.random.normal(ks[2], (DEPTH, P_IN), f32)).at[:, OFF_F:OFF_B].add(
        jnp.linspace(3.0, 6.0, N_MLSTM_HEADS, dtype=f32))
    conv_w = jax.random.normal(ks[3], (DEPTH, CONV_WIDTH, D_CONV), f32) * (CONV_WIDTH ** -0.5)
    mh_norm_g = 1.0 + 0.02 * jax.random.normal(ks[4], (DEPTH, D_MLSTM), f32)
    w_out = jax.random.normal(ks[5], (DEPTH, D_MIX, D_MODEL), f32) * (D_MIX ** -0.5) * BETA
    ln_mix_g = 1.0 + 0.02 * jax.random.normal(ks[6], (DEPTH, D_MODEL), f32)
    ln_mix_b = 0.02 * jax.random.normal(ks[7], (DEPTH, D_MODEL), f32)
    router_w = jax.random.normal(ks[8], (D_MODEL, N_EXPERTS), f32) * (D_MODEL ** -0.5)
    router_b = 0.01 * jax.random.normal(ks[9], (N_EXPERTS,), f32)
    w_gate = jax.random.normal(ks[10], (DEPTH, N_EXPERTS, D_MODEL, D_FF_EXPERT), f32) * (D_MODEL ** -0.5)
    w_up = jax.random.normal(ks[11], (DEPTH, N_EXPERTS, D_MODEL, D_FF_EXPERT), f32) * (D_MODEL ** -0.5)
    w_down = jax.random.normal(ks[12], (DEPTH, N_EXPERTS, D_FF_EXPERT, D_MODEL), f32) * (D_FF_EXPERT ** -0.5) * BETA
    ln_moe_g = 1.0 + 0.02 * jax.random.normal(ks[13], (DEPTH, D_MODEL), f32)
    ln_moe_b = 0.02 * jax.random.normal(ks[14], (DEPTH, D_MODEL), f32)
    return {"x": x, "w_in": w_in, "b_in": b_in, "conv_w": conv_w, "mh_norm_g": mh_norm_g, "w_out": w_out,
            "ln_mix_g": ln_mix_g, "ln_mix_b": ln_mix_b, "router_w": router_w, "router_b": router_b,
            "w_gate": w_gate, "w_up": w_up, "w_down": w_down, "ln_moe_g": ln_moe_g, "ln_moe_b": ln_moe_b}

def reference(x, w_in, b_in, conv_w, mh_norm_g, w_out, ln_mix_g, ln_mix_b, router_w, router_b,
              w_gate, w_up, w_down, ln_moe_g, ln_moe_b):
    for l in range(DEPTH):
        mix = hybrid_mixer(x, w_in[l], b_in[l], conv_w[l], mh_norm_g[l], w_out[l])
        x = layer_norm(ALPHA * x + mix, ln_mix_g[l], ln_mix_b[l])
        ffn = grouped_moe(x, router_w, router_b, w_gate[l], w_up[l], w_down[l])
        x = layer_norm(ALPHA * x + ffn, ln_moe_g[l], ln_moe_b[l])
    return x


_drawn_inputs = setup_inputs


def setup_inputs(seed=0):
    import zlib

    import numpy as np

    out = dict(_drawn_inputs(seed))
    spreads = {}
    factors = {'mh_norm_g': 3.752, 'ln_moe_g': 2.744, 'ln_moe_b': 2.873}
    for name, (base, spread) in spreads.items():
        noise = np.random.default_rng([zlib.crc32(name.encode()), seed]).standard_normal(out[name].shape)
        drawn = base * np.exp(spread * noise) if base else spread * noise
        out[name] = __import__('jax').numpy.asarray(drawn.astype(out[name].dtype))
    for name, factor in factors.items():
        out[name] = (out[name] * factor).astype(out[name].dtype)
    return out
```

```python
import concourse.bass as bass
from concourse import mybir
from contextlib import ExitStack

P = 128
F32 = mybir.dt.float32
F32R = mybir.dt.float32r
BF16 = mybir.dt.bfloat16
I32 = mybir.dt.int32
ALU = mybir.AluOpType
ACT = mybir.ActivationFunctionType
AX = mybir.AxisListType

LN_EPS = 1e-5
BANK = 512
MASKED = -1e30
LOWEST = -3e38


def tensors(nc, ctx, stage):
    def sb(name, shape, dt=F32):
        return ctx.enter_context(nc.sbuf_tensor(f"{stage}_{name}", shape, dt))

    def ps(name, shape, dt=F32):
        return ctx.enter_context(nc.psum_tensor(f"{stage}_{name}", shape, dt))

    def sem(name):
        return ctx.enter_context(nc.semaphore(f"{stage}_{name}"))

    return sb, ps, sem


def wait_apart(engine, carrier, sem, value):
    engine.wait_ge(sem, value)
    engine.sem_inc(carrier, 1)


class Order:

    def __init__(self, engine, sem, per_turn, before=0):
        self.engine, self.sem, self.per_turn, self.before, self.n = engine, sem, per_turn, before, 0

    def step(self, instruction):
        self.n += 1
        instruction.then_inc(self.sem, 1)

    def due(self, turn=0):
        return self.sem, turn * self.per_turn + self.before + self.n

    def wait(self, turn=0):
        self.engine.wait_ge(*self.due(turn))


def mixer(nc, keep, x, w_in, b_in, conv_w, mh_g, w_out, ln_g, ln_b, x1_dram, acc_dram, alpha):
    S, D = x.shape
    DM = w_out.shape[0] // 2
    NH = 4
    DH = DM // NH
    TAPS = conv_w.shape[0]
    GT = BANK
    NG = S // GT
    NT = GT // P
    KC = D // P
    KH = KC // 2
    OFF_I = 4 * DM
    OFF_F = OFF_I + NH
    OFF_B = OFF_F + NH
    OFF_C = OFF_B + DM
    OFF_X = OFF_C + DM
    QB, KB, VB, OB, CB, XB, BB, OUT0, OUT1 = range(9)
    BLOCK_COL = {QB: 0, KB: DM, VB: 2 * DM, OB: 3 * DM, CB: OFF_C, XB: OFF_X, BB: OFF_B, OUT0: 0, OUT1: BANK}
    BY_CHANNEL = (QB, KB, CB, XB, BB)
    BY_ACT = (QB, CB)
    NB = 9
    ST = 2 * NB
    FULL = NB * NT
    N_ACT = len(BY_ACT) * NT
    N_DVE = FULL - N_ACT
    assert DH == P and D == 2 * BANK and DM == BANK and NT == NH and TAPS == 3
    W = DH + 1

    SLOT = {}
    for c in range(NT):
        for k in range(3):
            n = 3 * c + k
            SLOT[(8 + n // 2, 2 * (n % 2))] = ("S1", "S2", "S3")[k], c
    SLOT[(14, 1)] = "Y", NT - 1
    for t in range(NT):
        SLOT[(15 + t // 2, 2 * (t % 2))] = "X", t

    def previous(b):
        return (b - 1) % NB

    def dve_count(b):
        return sum(1 for k in range(b) if k not in BY_ACT)

    def act_count(b):
        return sum(1 for k in range(b) if k in BY_ACT)

    ctx = ExitStack()
    with ctx:
        sb, ps, sem = tensors(nc, ctx, "mix")
        xTh, xTl = (sb(n, [P, KC, GT], F32R) for n in ("xT_high", "xT_low"))
        yTh, yTl = (sb(n, [P, KC, GT], F32R) for n in ("yT_high", "yT_low"))
        raw = sb("w_raw", [P, 2, KH, BANK])
        wh, wl = (sb(n, [P, 2, KH, BANK], F32R) for n in ("w_high", "w_low"))
        wgr = sb("w_gates_raw", [P, KC, 2 * NH])
        GC = 32 + NH
        wgh, wgl = (sb(n, [P, (KC - 1) * GC + P], F32R) for n in ("w_gates_high", "w_gates_low"))
        gates_h, gates_l = (w[:, 0:KC * GC].rearrange("p (c n) -> p c n", c=KC) for w in (wgh, wgl))
        qT = sb("qT", [P, NH, GT])
        kT = sb("kT", [P, NH, GT])
        V = sb("values", [P, NT, NH, W])
        OG = sb("o_gate", [P, NT, DM])
        CUR = sb("conv_or_residual", [P, NT * GT + NT * (GT + 2)])
        CT = CUR[:, 0:NT * GT].rearrange("p (t n) -> p t n", t=NT)
        U = CUR[:, NT * GT:].rearrange("p (t n) -> p t n", t=NT)
        R = CUR[:, 0:NT * D].rearrange("p (t n) -> p t n", t=NT)
        halo = sb("u_halo", [P, NT, 2])
        XN = sb("x_rows", [P, 2, D])
        IG, FF, BR, CM = (sb(n, [NH, GT]) for n in ("row_i", "row_f", "row_b", "row_max"))
        MS = sb("row_m", [NH, NT + 1])
        GM = sb("row_g", [NH, NT])
        SPR = sb("row_decay", [NH, NT])
        ROWS = sb("rows", [P, GT])
        NAT = sb("columns", [P, NT, 4, NH])
        SPB = sb("decay", [P, NH, NT])
        DT = sb("decayed_scores", [P, NH, P])
        KE = sb("k_weighted", [P, NH, DH])
        YC = KE[:].rearrange("p h n -> p (h n)")
        NU = sb("numerator", [P, NH, W])
        CS = sb("state", [P, NH, W])
        den = sb("denominator", [P, NH])
        stat = sb("head_stats", [P, NH, 6])
        mv = sb("head_mean_var", [P, NH, 2])
        rstd = sb("head_rstd", [P, NH])
        lstat = sb("ln_stats", [P, NT, 2, 6])
        lmv = sb("ln_mean_var", [P, NT, 2])
        lrs = sb("ln_rstd", [P, NT])
        ident = keep.ident
        identb = sb("ident_bf16", [P, P], BF16)
        mask = sb("causal_mask", [P, P], BF16)
        sel = sb("head_select", [NH, NH, P])
        zrow = sb("zero_row", [NH, P])
        bq, bk, bc_, bx, bb = (sb(n, [P, NT]) for n in ("b_q", "b_k", "b_c", "b_x", "b_b"))
        bi, bf = (sb(n, [NH, 1]) for n in ("b_i", "b_f"))
        eps = sb("eps", [P, 1])
        cw = sb("conv_taps", [P, TAPS, NT])
        bv, bo = (sb(n, [P, DM]) for n in ("b_v", "b_o"))
        mhg = sb("mh_gain", [P, NH])
        lng, lnb = (sb(n, [P, D]) for n in ("ln_gain", "ln_bias"))

        acc = [ps(f"acc{t}", [P, BANK]) for t in range(NT)]
        aux = [ps(f"aux{t}", [P, BANK]) for t in range(4)]

        consts_in = sem("consts_in")
        gates_w_in = sem("gates_w_in")
        consts_made = sem("consts_made")
        dve_consts = sem("dve_consts")
        gates_w_split = sem("gates_w_split")
        raw_in = [sem(f"w_raw_in{k}") for k in range(2)]
        split_h = sem("w_high_ready")
        split_l = sem("w_low_ready")
        stage_used = sem("stage_used")
        x_in = [sem(f"x_rows_in{k}") for k in range(2)]
        xt_ps = sem("xT_in_psum")
        xt_h = sem("xT_high_ready")
        xt_done = sem("xT_ready")
        acc_full = sem("acc_full")
        act_out = sem("acc_taken_by_act")
        dve_out = sem("acc_taken_by_dve")
        gates_ps = sem("gates_in_psum")
        f_neg = sem("f_neg_ready")
        f_log = sem("f_log_ready")
        exps_in = sem("row_exponents_ready")
        rows_done = sem("rows_ready")
        nat_ps = sem("columns_in_psum")
        nat_done = sem("columns_ready")
        o_gate = sem("o_gate_ready")
        s1_ps = sem("scores_in_psum")
        dt_done = sem("decay_matrix_ready")
        pt_done = sem("weights_ready")
        num_ps = sem("numerators_in_psum")
        inter_done = sem("state_part_taken")
        num_done = sem("numerators_taken")
        var_done = sem("head_var_ready")
        rs_done = sem("head_rstd_ready")
        y_done = sem("y_ready")
        cl_ps = sem("chunk_state_in_psum")
        state_done = sem("state_updated")
        y_ps = sem("yT_in_psum")
        yh_done = sem("yT_high_ready")
        yl_done = sem("yT_low_ready")
        ych_done = sem("y_conv_high_ready")
        conv_done = sem("conv_group_done")
        res_in = [sem(f"residual_in{t}") for t in range(NT)]
        lvar_done = sem("ln_var_ready")
        lrs_done = sem("ln_rstd_ready")
        ln_done = sem("ln_normalised")
        x1_out = sem("x1_stored")
        xa_out = sem("alpha_x1_stored")
        dve_own = sem("dve_own")
        act_own = sem("act_own")
        pool_own = sem("pool_own")
        pool_idle = sem("pool_wait_carrier")
        dve_idle = sem("dve_wait_carrier")

        N_CONSTS = (6 + TAPS + 2 + 4) * 16

        def w_view(stage):
            b, half = stage // 2, stage % 2
            src = w_out if b >= OUT0 else w_in
            col = BLOCK_COL[b]
            return src[half * KH * P:(half + 1) * KH * P, col:col + BANK].rearrange("(c p) n -> p c n", p=P)

        def column(v):
            return v.rearrange("(t p) -> p t", p=P)

        block = ctx.enter_context(nc.Block())

        @block.sync
        def _(sp):
            def load_stage(g, stage, after):
                n = g * ST + stage + after * ST
                if after or stage:
                    sp.wait_ge(split_l, n - 1)
                sp.dma_start(raw[:, stage % 2], w_view(stage)).then_inc(raw_in[stage % 2], 16)

            sp.dma_start(wgr[:], w_in[:, OFF_I:OFF_B].rearrange("(c p) n -> p c n", p=P)).then_inc(gates_w_in, 16)
            load_stage(0, 0, 0)
            for dst, off in ((bq, 0), (bk, DM), (bc_, OFF_C), (bx, OFF_X), (bb, OFF_B)):
                sp.dma_start(dst[:], column(b_in[off:off + DM]), allow_slow_non_contiguous=True).then_inc(consts_in, 16)
            sp.dma_start(mhg[:], column(mh_g), allow_slow_non_contiguous=True).then_inc(consts_in, 16)
            for k in range(TAPS):
                sp.dma_start(cw[:, k, :], column(conv_w[k]), allow_slow_non_contiguous=True).then_inc(consts_in, 16)
            sp.dma_start(bi[:], b_in[OFF_I:OFF_F].rearrange("(h a) -> h a", a=1)).then_inc(consts_in, 16)
            sp.dma_start(bf[:], b_in[OFF_F:OFF_B].rearrange("(h a) -> h a", a=1)).then_inc(consts_in, 16)
            for dst, v in ((bv, b_in[2 * DM:3 * DM]), (bo, b_in[3 * DM:4 * DM]), (lng, ln_g), (lnb, ln_b)):
                sp.dma_start(dst[:], v.partition_broadcast(P)).then_inc(consts_in, 16)
            with sp.Fori(0, NG) as g:
                for stage in range(1, ST):
                    load_stage(g, stage, 0)
                load_stage(g, 0, 1)

        POOL_TURN = 3 * NT

        @block.gpsimd
        def _(pool):
            own = Order(pool, pool_own, POOL_TURN)
            for n in range(2):
                pool.dma_start(XN[:, n], x[n * P:(n + 1) * P]).then_inc(x_in[n], 16)
            pool.memset(ident[:], 0.0).then_inc(consts_made, 1)
            pool.memset(mask[:], 0.0).then_inc(consts_made, 1)
            pool.memset(sel[:], 0.0).then_inc(consts_made, 1)
            pool.memset(identb[:], 0.0).then_inc(consts_made, 1)
            pool.wait_ge(consts_made, 4)
            for t in (ident, identb):
                pool.affine_select(out=t[:], in_=t[:], compare_op=ALU.not_equal, fill=1.0, base=0,
                                   pattern=[[-1, P]], channel_multiplier=1).then_inc(consts_made, 1)
            pool.affine_select(out=mask[:], in_=mask[:], compare_op=ALU.is_ge, fill=MASKED, base=0,
                               pattern=[[1, P]], channel_multiplier=-1).then_inc(consts_made, 1)
            pool.affine_select(out=sel[:], in_=sel[:], compare_op=ALU.not_equal, fill=1.0, base=0,
                               pattern=[[-1, NH], [0, P]], channel_multiplier=1).then_inc(consts_made, 1)
            for n in range(2, NT):
                pool.wait_ge(xt_ps, n - 1)
                pool.dma_start(XN[:, n % 2], x[n * P:(n + 1) * P]).then_inc(x_in[n % 2], 16)
            pool.wait_ge(consts_in, N_CONSTS)
            with pool.Fori(0, NG) as g:
                for t in range(NT):
                    if t == 0:
                        wait_apart(pool, pool_idle, conv_done, (g + 1) * NT)
                    pool.dma_start(R[:, t], x[bass.ds(g * GT + t * P, P)]).then_inc(res_in[t], 16)
                for t in range(NT):
                    wait_apart(pool, pool_idle, xt_ps, g * NT + NT + t - 1)
                    row = (g + 1) % NG * GT + t * P
                    pool.dma_start(XN[:, t % 2], x[bass.ds(row, P)]).then_inc(x_in[t % 2], 16)
                for t in range(NT):
                    pool.wait_ge(ln_done, g * NT + t + 1)
                    own.step(pool.tensor_tensor(R[:, t], R[:, t], lng[:], ALU.mult))
                    own.wait(g)
                    own.step(pool.tensor_tensor(R[:, t], R[:, t], lnb[:], ALU.add))
                    wait_apart(pool, pool_idle, *own.due(g))
                    row = g * GT + t * P
                    pool.dma_start(x1_dram[bass.ds(row, P)], R[:, t]).then_inc(x1_out, 16)
                    wait_apart(pool, pool_idle, x1_out, (g * NT + t + 1) * 16)
                    own.step(pool.tensor_scalar(R[:, t], R[:, t], alpha, None, ALU.mult))
                    wait_apart(pool, pool_idle, *own.due(g))
                    pool.dma_start(acc_dram[bass.ds(row, P)], R[:, t]).then_inc(xa_out, 16)
            assert own.n == POOL_TURN
            pool.wait_ge(x1_out, NG * NT * 16)
            pool.wait_ge(xa_out, NG * NT * 16)

        ACT_TURN = 1 + NT + 1 + 2 * NT

        @block.scalar
        def _(act):
            own = Order(act, act_own, ACT_TURN)

            def split_stage(g, stage, after):
                n = g * ST + stage + after * ST
                use = g * NB + stage // 2 + after * NB
                act.wait_ge(raw_in[stage % 2], (use + 1) * 16)
                if stage % 2:
                    act.wait_ge(acc_full, g * FULL + stage // 2 * NT + after * FULL)
                else:
                    act.wait_ge(stage_used, use)
                act.activation(wh[:, stage % 2], raw[:, stage % 2], ACT.Copy).then_inc(split_h, 1)

            def take(g, stage):
                b = stage // 2
                if b not in BY_ACT or stage % 2 == 0:
                    if b == BB and stage % 2:
                        for t in range(NT):
                            act.wait_ge(dve_out, g * N_DVE + dve_count(BB) * NT + t + 1)
                            act.activation(yTh[:, NH + t], YC, ACT.Copy).then_inc(ych_done, 1)
                    return
                for t in range(NT):
                    act.wait_ge(acc_full, g * FULL + b * NT + t + 1)
                    if b == QB:
                        act.activation(qT[:, t], acc[t][:], ACT.Identity, bias=bq[:, t:t + 1]).then_inc(act_out, 1)
                    else:
                        if t == 0:
                            act.wait_ge(xa_out, g * NT * 16)
                        act.activation(CT[:, t], acc[t][:], ACT.Identity, bias=bc_[:, t:t + 1]).then_inc(act_out, 1)

            def xt_tile(g, t, after):
                act.wait_ge(xt_ps, g * NT + t + 1 + after * NT)
                for k in range(2):
                    ins = act.activation(xTh[:, 4 * k:4 * k + 4, t * P:(t + 1) * P],
                                         aux[2 * (t % 2) + k][:].rearrange("p (c n) -> p c n", c=4), ACT.Copy)
                ins.then_inc(xt_h, 1)

            def extra(g, what, c):
                if what == "S1":
                    act.wait_ge(s1_ps, g * NT + c + 1)
                    for h in range(NH):
                        ins = act.activation(DT[:, h], aux[0][:, h * P:(h + 1) * P], ACT.Exp,
                                             bias=NAT[:, c, 3, h:h + 1])
                    ins.then_inc(dt_done, 1)
                if what == "Y" or (what == "S1" and c > 0):
                    cy = c if what == "Y" else c - 1
                    act.wait_ge(y_ps, g * NT + cy + 1)
                    a = aux[0] if what == "Y" else aux[3]
                    for h in range(NH):
                        ins = act.activation(yTh[:, h, cy * P:(cy + 1) * P], a[:, h * P:(h + 1) * P],
                                             ACT.Copy, scale=mhg[:, h:h + 1])
                    ins.then_inc(yh_done, 1)
                if what == "S2":
                    act.wait_ge(num_ps, g * NT + c + 1)
                    act.wait_ge(y_ps, g * NT + c)
                    for h in range(NH):
                        o = (h % 2) * W
                        ins = act.activation(NU[:, h], aux[2 + h // 2][:, o:o + W], ACT.Copy,
                                             scale=NAT[:, c, 0, h:h + 1])
                    ins.then_inc(inter_done, 1)
                    act.wait_ge(var_done, g * NT + c + 1)
                    own.step(act.activation(rstd[:], mv[:, :, 1], ACT.Ln, bias=eps[:, 0:1]))
                    own.wait(g)
                    act.activation(rstd[:], rstd[:], ACT.Exp, scale=-0.5).then_inc(rs_done, 1)
                if what == "X":
                    xt_tile(g, c, 1)

            act.wait_ge(gates_w_in, 16)
            act.wait_ge(gates_w_split, 2)
            act.activation(gates_h[:, :, 0:NH], wgr[:, :, 0:NH], ACT.Copy)
            act.activation(gates_h[:, :, 32:], wgr[:, :, NH:], ACT.Copy).then_inc(gates_w_split, 1)
            split_stage(0, 0, 0)
            act.wait_ge(consts_made, 8)
            for t in range(NT):
                xt_tile(0, t, 0)
            act.wait_ge(dve_consts, 1)
            act.wait_ge(consts_in, N_CONSTS)
            with act.Fori(0, NG) as g:
                for stage in range(ST):
                    if stage > 0:
                        take(g, stage - 1)
                    if stage == 0:
                        act.wait_ge(f_neg, g + 1)
                        own.step(act.activation(CM[:], CM[:], ACT.Exp))
                        own.wait(g)
                        act.activation(CM[:], CM[:], ACT.Ln, bias=1.0).then_inc(f_log, 1)
                    if stage == 2:
                        act.wait_ge(exps_in, g + 1)
                        act.activation(ROWS[0:NH], ROWS[0:NH], ACT.Exp)
                        act.activation(ROWS[32:32 + NH], ROWS[32:32 + NH], ACT.Exp, scale=-1.0)
                        act.activation(ROWS[64:64 + NH], ROWS[64:64 + NH], ACT.Exp)
                        act.activation(SPR[:], SPR[:], ACT.Exp).then_inc(rows_done, 1)
                    if (stage, 0) in SLOT:
                        extra(g, *SLOT[(stage, 0)])
                    split_stage(g, (stage + 1) % ST, (stage + 1) // ST)
                    if stage == 8:
                        for t in range(NT):
                            act.wait_ge(dve_out, g * N_DVE + dve_count(OB) * NT + t + 1)
                            own.step(act.activation(OG[:, t], OG[:, t], ACT.Exp, scale=-1.0))
                        own.wait(g)
                        for t in range(NT):
                            own.step(act.activation(OG[:, t], OG[:, t], ACT.Ln, bias=1.0))
                        own.wait(g)
                        for t in range(NT):
                            act.activation(OG[:, t], OG[:, t], ACT.Exp, scale=-1.0).then_inc(o_gate, 1)
                    for t in range(1, NT):
                        if (stage, t) in SLOT:
                            extra(g, *SLOT[(stage, t)])
                own_ln = own
                act.wait_ge(lvar_done, g + 1)
                own_ln.step(act.activation(lrs[:], lmv[:, :, 1], ACT.Ln, bias=eps[:, 0:1]))
                own_ln.wait(g)
                act.activation(lrs[:], lrs[:], ACT.Exp, scale=-0.5).then_inc(lrs_done, 1)
            assert own.n == ACT_TURN, own.n

        DVE_TURN = 55
        DVE_BEFORE = 0

        @block.vector
        def _(dve):
            own = Order(dve, dve_own, DVE_TURN, DVE_BEFORE)

            def split_stage(g, stage, after):
                n = g * ST + stage + after * ST
                dve.wait_ge(split_h, n + 1)
                dve.tensor_tensor(wl[:, stage % 2], raw[:, stage % 2], wh[:, stage % 2].bitcast(F32),
                                  ALU.subtract).then_inc(split_l, 1)

            def take(g, stage):
                b = stage // 2
                if stage % 2 == 0 or b in BY_ACT:
                    return
                for t in range(NT):
                    dve.wait_ge(acc_full, g * FULL + b * NT + t + 1)
                    a = acc[t][:]
                    ah = acc[t][:].rearrange("p (h n) -> p h n", h=NH)
                    if b == KB:
                        dve.tensor_scalar(kT[:, t], a, bk[:, t:t + 1], DH ** -0.5, ALU.add, ALU.mult)\
                           .then_inc(dve_out, 1)
                    elif b == VB:
                        dve.tensor_tensor(V[:, t, :, 0:DH], ah, bv[:].rearrange("p (h n) -> p h n", h=NH),
                                          ALU.add).then_inc(dve_out, 1)
                    elif b == OB:
                        dve.tensor_tensor(OG[:, t], a, bo[:], ALU.add).then_inc(dve_out, 1)
                    elif b == XB:
                        dve.scalar_tensor_tensor(out=U[:, t, 2:], in0=a, scalar=bx[:, t:t + 1], in1=CT[:, t],
                                                 op0=ALU.add, op1=ALU.mult).then_inc(dve_out, 1)
                        own.step(dve.tensor_copy(U[:, t, 0:2], halo[:, t]))
                        dve.wait_ge(dve_out, g * N_DVE + dve_count(b) * NT + t + 1)
                        own.wait(g)
                        own.step(dve.tensor_copy(halo[:, t], U[:, t, GT:]))
                        own.step(dve.tensor_scalar(CT[:, t], U[:, t, 0:GT], cw[:, 0, t:t + 1], None, ALU.mult))
                        for k in range(1, TAPS):
                            own.wait(g)
                            own.step(dve.scalar_tensor_tensor(out=CT[:, t], in0=U[:, t, k:k + GT],
                                                              scalar=cw[:, k, t:t + 1], in1=CT[:, t],
                                                              op0=ALU.mult, op1=ALU.add))
                    elif b == BB:
                        if t:
                            dve.wait_ge(conv_done, g * NT + t)
                        dve.scalar_tensor_tensor(out=YC, in0=a, scalar=bb[:, t:t + 1], in1=CT[:, t],
                                                 op0=ALU.add, op1=ALU.mult).then_inc(dve_out, 1)
                        dve.wait_ge(ych_done, g * NT + t + 1)
                        dve.tensor_tensor(yTl[:, NH + t], YC, yTh[:, NH + t].bitcast(F32), ALU.subtract)\
                           .then_inc(conv_done, 1)
                    else:
                        n0 = (b - OUT0) * BANK
                        if b == OUT0:
                            dve.wait_ge(res_in[t], (g + 1) * 16)
                        dve.scalar_tensor_tensor(out=R[:, t, n0:n0 + BANK], in0=R[:, t, n0:n0 + BANK], scalar=alpha,
                                                 in1=a, op0=ALU.mult, op1=ALU.add).then_inc(dve_out, 1)

            def xt_tile(g, t, after):
                dve.wait_ge(xt_h, g * NT + t + 1 + after * NT)
                for k in range(2):
                    sl = (slice(None), slice(4 * k, 4 * k + 4), slice(t * P, (t + 1) * P))
                    ins = dve.tensor_tensor(xTl[sl], aux[2 * (t % 2) + k][:].rearrange("p (c n) -> p c n", c=4),
                                            xTh[sl].bitcast(F32), ALU.subtract)
                ins.then_inc(xt_done, 1)

            def extra(g, what, c):
                if what == "S1":
                    dve.wait_ge(s1_ps, g * NT + c + 1)
                    dve.tensor_tensor(KE[:], aux[2][:].rearrange("p (h n) -> p h n", h=NH),
                                      NAT[:, c, 2].unsqueeze(2).to_broadcast([P, NH, DH]), ALU.mult)
                    dve.wait_ge(dt_done, g * NT + c + 1)
                    dve.tensor_tensor(DT[:], DT[:], aux[1][:].rearrange("p (h n) -> p h n", h=NH),
                                      ALU.mult).then_inc(pt_done, 1)
                if what == "Y" or (what == "S1" and c > 0):
                    cy = c if what == "Y" else c - 1
                    dve.wait_ge(yh_done, g * NT + cy + 1)
                    a = aux[0] if what == "Y" else aux[3]
                    for h in range(NH):
                        sl = (slice(None), h, slice(cy * P, (cy + 1) * P))
                        ins = dve.scalar_tensor_tensor(out=yTl[sl], in0=a[:, h * P:(h + 1) * P],
                                                       scalar=mhg[:, h:h + 1], in1=yTh[sl].bitcast(F32),
                                                       op0=ALU.mult, op1=ALU.subtract)
                    ins.then_inc(yl_done, 1)
                if what == "S2":
                    dve.wait_ge(inter_done, g * NT + c + 1)
                    for k in range(2):
                        ins = dve.tensor_tensor(NU[:, 2 * k:2 * k + 2], NU[:, 2 * k:2 * k + 2],
                                                aux[k][:, 0:2 * W].rearrange("p (h n) -> p h n", h=2), ALU.add)
                    ins.then_inc(num_done, 1)
                    dve.wait_ge(num_done, g * NT + c + 1)
                    own.step(dve.scalar_tensor_tensor(out=den[:], in0=NU[:, :, DH], scalar=-1.0, in1=NU[:, :, DH],
                                                      op0=ALU.mult, op1=ALU.max))
                    own.wait(g)
                    own.step(dve.tensor_tensor(den[:], den[:], NAT[:, c, 1], ALU.max))
                    own.wait(g)
                    own.step(dve.reciprocal(den[:], den[:]))
                    own.wait(g)
                    own.step(dve.tensor_tensor(NU[:, :, 0:DH], NU[:, :, 0:DH],
                                               den[:].unsqueeze(2).to_broadcast([P, NH, DH]), ALU.mult))
                    own.wait(g)
                    for h in range(NH):
                        ins = dve.bn_stats(stat[:, h], NU[:, h, 0:DH])
                    own.step(ins)
                    wait_apart(dve, dve_idle, *own.due(g))
                    for h in range(NH):
                        ins = dve.bn_aggr(mv[:, h], stat[:, h])
                    ins.then_inc(var_done, 1)
                    dve.wait_ge(rs_done, g * NT + c + 1)
                    for h in range(NH):
                        ins = dve.tensor_scalar(NU[:, h, 0:DH], NU[:, h, 0:DH], mv[:, h, 0:1], rstd[:, h:h + 1],
                                                ALU.subtract, ALU.mult)
                    own.step(ins)
                    own.wait(g)
                    dve.wait_ge(o_gate, g * NT + c + 1)
                    dve.tensor_tensor(NU[:, :, 0:DH], NU[:, :, 0:DH], OG[:, c].rearrange("p (h n) -> p h n", h=NH),
                                      ALU.mult).then_inc(y_done, 1)
                if what == "S3":
                    dve.wait_ge(cl_ps, g * NT + c + 1)
                    for h in range(NH):
                        o = (h % 2) * W
                        ins = dve.scalar_tensor_tensor(out=CS[:, h], in0=CS[:, h], scalar=SPB[:, h, c:c + 1],
                                                       in1=aux[2 + h // 2][:, o:o + W], op0=ALU.mult, op1=ALU.add)
                    ins.then_inc(state_done, 1)
                if what == "X":
                    xt_tile(g, c, 1)

            for t in (wgh, wgl):
                dve.memset(t[:].bitcast(F32), 0.0).then_inc(gates_w_split, 1)
            dve.memset(zrow[:], 0.0)
            dve.memset(eps[:], LN_EPS)
            dve.memset(halo[:], 0.0)
            dve.memset(CS[:], 0.0)
            dve.memset(ROWS[:], 0.0)
            dve.memset(MS[:], 0.0)
            dve.memset(V[:, :, :, DH:], 1.0).then_inc(dve_consts, 1)
            dve.wait_ge(gates_w_split, 3)
            dve.tensor_tensor(gates_l[:, :, 0:NH], wgr[:, :, 0:NH], gates_h[:, :, 0:NH].bitcast(F32), ALU.subtract)
            dve.tensor_tensor(gates_l[:, :, 32:], wgr[:, :, NH:], gates_h[:, :, 32:].bitcast(F32), ALU.subtract).then_inc(gates_w_split, 1)
            split_stage(0, 0, 0)
            for t in range(NT):
                xt_tile(0, t, 0)
            dve.wait_ge(dve_consts, 1)
            dve.wait_ge(consts_in, N_CONSTS)
            with dve.Fori(0, NG) as g:
                for stage in range(ST):
                    if stage > 0:
                        take(g, stage - 1)
                    if stage == 0:
                        dve.wait_ge(gates_ps, g + 1)
                        dve.tensor_scalar(IG[:], aux[0][0:NH], bi[:, 0:1], None, ALU.add)
                        own.step(dve.tensor_scalar(FF[:], aux[0][32:32 + NH], bf[:, 0:1], None, ALU.add))
                        own.wait(g)
                        dve.scalar_tensor_tensor(out=CM[:], in0=FF[:], scalar=-1.0, in1=FF[:], op0=ALU.mult,
                                                 op1=ALU.min).then_inc(f_neg, 1)
                    if stage == 1:
                        dve.wait_ge(f_log, g + 1)
                        own.step(dve.scalar_tensor_tensor(out=FF[:], in0=FF[:], scalar=0.0, in1=CM[:], op0=ALU.min,
                                                          op1=ALU.subtract))
                        own.wait(g)
                        for c in range(NT):
                            s = slice(c * P, (c + 1) * P)
                            ins = dve.tensor_tensor_scan(FF[:, s], FF[:, s], zrow[:], 0.0, ALU.add, ALU.add)
                        own.step(ins)
                        own.wait(g)
                        own.step(dve.tensor_tensor(BR[:], IG[:], FF[:], ALU.subtract))
                        own.wait(g)
                        for c in range(NT):
                            s = slice(c * P, (c + 1) * P)
                            ins = dve.tensor_tensor_scan(CM[:, s], BR[:, s], zrow[:], LOWEST, ALU.max, ALU.add)
                        own.step(ins)
                        own.step(dve.tensor_copy(ROWS[96:96 + NH], BR[:]))
                        own.wait(g)
                        last = FF[:].rearrange("h (c n) -> h c n", c=NT)[:, :, P - 1]
                        bmax = CM[:].rearrange("h (c n) -> h c n", c=NT)[:, :, P - 1]
                        dve.wait_ge(exps_in, g)
                        own.step(dve.tensor_tensor_scan(MS[:, 1:], bmax, last, MS[:, 0:1], ALU.max, ALU.add))
                        own.wait(g)
                        before = MS[:, 0:NT].unsqueeze(2).to_broadcast([NH, NT, P])
                        cm3 = CM[:].rearrange("h (c n) -> h c n", c=NT)
                        own.step(dve.tensor_tensor(cm3, cm3, before, ALU.max))
                        own.step(dve.tensor_tensor(GM[:], last, MS[:, 1:], ALU.subtract))
                        own.wait(g)
                        dve.tensor_tensor(ROWS[0:NH].rearrange("h (c n) -> h c n", c=NT), before, cm3, ALU.subtract)
                        dve.tensor_tensor(ROWS[32:32 + NH], FF[:], CM[:], ALU.add)
                        dve.tensor_tensor(ROWS[64:64 + NH].rearrange("h (c n) -> h c n", c=NT),
                                          BR[:].rearrange("h (c n) -> h c n", c=NT),
                                          GM[:].unsqueeze(2).to_broadcast([NH, NT, P]), ALU.add)
                        dve.tensor_scalar(IG[:], CM[:], -1.0, None, ALU.mult)
                        own.step(dve.tensor_tensor(SPR[:], GM[:], MS[:, 0:NT], ALU.add))
                        own.wait(g)
                        dve.tensor_copy(MS[:, 0:1], MS[:, NT:]).then_inc(exps_in, 1)
                    if stage == 4:
                        dve.wait_ge(nat_ps, g + 1)
                        dve.tensor_copy(NAT[:], aux[3][:].rearrange("p (c q n) -> p c q n", c=NT, q=4)[:, :, :, 0:NH])
                        dve.tensor_copy(SPB[:], aux[1][:, 0:NH * NT].rearrange("p (h c) -> p h c", h=NH))\
                           .then_inc(nat_done, 1)
                    if (stage, 0) in SLOT:
                        extra(g, *SLOT[(stage, 0)])
                    split_stage(g, (stage + 1) % ST, (stage + 1) // ST)
                    for t in range(1, NT):
                        if (stage, t) in SLOT:
                            extra(g, *SLOT[(stage, t)])
                take(g, ST - 1)
                dve.wait_ge(dve_out, (g + 1) * N_DVE)
                for t in range(NT):
                    for k in range(2):
                        ins = dve.bn_stats(lstat[:, t, k], R[:, t, k * BANK:(k + 1) * BANK])
                own.step(ins)
                wait_apart(dve, dve_idle, *own.due(g))
                for t in range(NT):
                    ins = dve.bn_aggr(lmv[:, t], lstat[:, t])
                ins.then_inc(lvar_done, 1)
                dve.wait_ge(lrs_done, g + 1)
                for t in range(NT):
                    dve.tensor_scalar(R[:, t], R[:, t], lmv[:, t, 0:1], lrs[:, t:t + 1], ALU.subtract, ALU.mult)\
                       .then_inc(ln_done, 1)
            assert own.n == DVE_TURN, own.n

        @block.tensor
        def _(pe):
            def three(out, ah, al, bh, bl, first, last):
                pe.matmul(out, ah, bh, start=first, stop=False)
                pe.matmul(out, ah, bl, start=False, stop=False)
                return pe.matmul(out, al, bh, start=False, stop=last)

            def tile(g, stage, t):
                b, half, s = stage // 2, stage % 2, stage % 2
                if half == 0:
                    if b == 0:
                        pe.wait_ge(dve_out, g * N_DVE)
                    elif previous(b) in BY_ACT:
                        pe.wait_ge(act_out, g * N_ACT + act_count(previous(b)) * NT + t + 1)
                    else:
                        pe.wait_ge(dve_out, g * N_DVE + dve_count(previous(b)) * NT + t + 1)
                sh, sl = (yTh, yTl) if b >= OUT0 else (xTh, xTl)
                for k in range(KH):
                    kc = half * KH + k
                    first, last = kc == 0, kc == KC - 1
                    cols = slice(t * P, (t + 1) * P)
                    if b in BY_CHANNEL:
                        ins = three(acc[t][:], wh[:, s, k, cols], wl[:, s, k, cols], sh[:, kc], sl[:, kc], first, last)
                    else:
                        ins = three(acc[t][:], sh[:, kc, cols], sl[:, kc, cols], wh[:, s, k], wl[:, s, k], first, last)
                if half:
                    ins.then_inc(acc_full, 1)
                elif t == NT - 1:
                    ins.then_inc(stage_used, 1)

            def xt_tile(g, t, after):
                n = g * NT + t + after * NT
                use = g * (NT // 2) + t // 2 + after * (NT // 2)
                pe.wait_ge(x_in[t % 2], (use + 1) * 16)
                if after and t < 2:
                    if t == 0:
                        pe.wait_ge(yl_done, g * NT + NT)
                    else:
                        pe.wait_ge(state_done, g * NT + NT)
                elif t >= 2:
                    pe.wait_ge(xt_done, n - 1)
                for k in range(KC):
                    ins = pe.transpose(aux[2 * (t % 2) + k // 4][:, (k % 4) * P:(k % 4 + 1) * P],
                                       XN[:, t % 2, k * P:(k + 1) * P], ident[:])
                ins.then_inc(xt_ps, 1)

            def extra(g, what, c):
                cols = slice(c * P, (c + 1) * P)
                if what == "S1":
                    if c == 0:
                        pe.wait_ge(nat_done, g + 1)
                    else:
                        pe.wait_ge(num_done, g * NT + c)
                        pe.wait_ge(state_done, g * NT + c)
                        pe.wait_ge(y_done, g * NT + c)
                        for h in range(NH):
                            ins = pe.transpose(aux[3][:, h * P:(h + 1) * P], NU[:, h, 0:DH], ident[:])
                        ins.then_inc(y_ps, 1)
                    for h in range(NH):
                        pe.matmul(aux[0][:, h * P:(h + 1) * P], identb[:], mask[:], start=True, stop=False)
                        pe.matmul(aux[0][:, h * P:(h + 1) * P], sel[:, h], IG[:, cols], start=False, stop=True)
                    for h in range(NH):
                        pe.matmul(aux[1][:, h * P:(h + 1) * P], kT[:, h, cols], qT[:, h, cols], start=True, stop=True)
                    for h in range(NH):
                        ins = pe.transpose(aux[2][:, h * P:(h + 1) * P], kT[:, h, cols], ident[:])
                    ins.then_inc(s1_ps, 1)
                if what == "S2":
                    pe.wait_ge(pt_done, g * NT + c + 1)
                    if c:
                        pe.wait_ge(yl_done, g * NT + c)
                    for h in range(NH):
                        o = (h % 2) * W
                        pe.matmul(aux[h // 2][:, o:o + W], DT[:, h], V[:, c, h], start=True, stop=True)
                    for h in range(NH):
                        o = (h % 2) * W
                        ins = pe.matmul(aux[2 + h // 2][:, o:o + W], qT[:, h, cols], CS[:, h], start=True, stop=True)
                    ins.then_inc(num_ps, 1)
                if what == "S3":
                    pe.wait_ge(num_done, g * NT + c + 1)
                    for h in range(NH):
                        o = (h % 2) * W
                        ins = pe.matmul(aux[2 + h // 2][:, o:o + W], KE[:, h], V[:, c, h], start=True, stop=True)
                    ins.then_inc(cl_ps, 1)
                if what == "Y":
                    pe.wait_ge(y_done, g * NT + c + 1)
                    for h in range(NH):
                        ins = pe.transpose(aux[0][:, h * P:(h + 1) * P], NU[:, h, 0:DH], ident[:])
                    ins.then_inc(y_ps, 1)
                if what == "X":
                    xt_tile(g, c, 1)

            pe.wait_ge(consts_made, 8)
            for t in range(NT):
                xt_tile(0, t, 0)
            pe.wait_ge(dve_consts, 1)
            pe.wait_ge(gates_w_split, 4)
            with pe.Fori(0, NG) as g:
                pe.wait_ge(xt_done, g * NT + NT)
                for k in range(KC):
                    ins = three(aux[0][:], wgh[:, k * GC:k * GC + P], wgl[:, k * GC:k * GC + P], xTh[:, k], xTl[:, k], k == 0, k == KC - 1)
                ins.then_inc(gates_ps, 1)
                for stage in range(ST):
                    pe.wait_ge(split_l, g * ST + stage + 1)
                    if stage == 4:
                        pe.wait_ge(rows_done, g + 1)
                        for c in range(NT):
                            pe.transpose(aux[3][:, c * P:(c + 1) * P], ROWS[:, c * P:(c + 1) * P], ident[:])
                        for h in range(NH):
                            ins = pe.matmul(aux[1][:, h * NT:(h + 1) * NT], sel[:, h], SPR[:], start=True, stop=True)
                        ins.then_inc(nat_ps, 1)
                    if stage == 14:
                        pe.wait_ge(conv_done, (g + 1) * NT)
                    if stage == 14:
                        pe.wait_ge(yl_done, g * NT + NT - 1)
                    for t in range(NT):
                        if stage == 14 and t == NT - 1:
                            pe.wait_ge(yl_done, g * NT + NT)
                        tile(g, stage, t)
                        if (stage, t) in SLOT:
                            extra(g, *SLOT[(stage, t)])
def route(nc, keep, x1_dram, acc_dram, router_w, router_b, n_groups):
    S, D = x1_dram.shape
    NE = router_w.shape[1]
    PG = NE // n_groups
    NT = S // P
    KC = D // P
    NBW = keep.gather.shape[1]
    TOP = 2

    ctx = ExitStack()
    with ctx:
        sb, ps, sem = tensors(nc, ctx, "route")
        X = sb("x1_rows", [P, 4, D])
        XT = sb("x1T", [P, 2, KC, P])
        RW = sb("router_w", [P, KC, NE])
        RB = sb("router_b", [P, NE])
        LG = sb("logits", [P, NT * NE])
        rows = sb("per_token", [P, 10, NT])
        HI, LO = (sb(n, [P, NT * n_groups, 2]) for n in ("pair_high", "pair_low"))
        G4 = sb("per_group", [P, 6, NT * n_groups])
        E16 = sb("per_expert", [P, 9, NT * NE])
        cnt = sb("per_count", [P, 4, NE])
        thr = sb("over_threshold", [P, NE, NT])
        slot_i = sb("slot_int", [P, 3, TOP * NT], I32)
        slot_f = sb("slot_parts", [P, 2, TOP * NT])
        gate = sb("gates", [P, TOP, NT])
        LOH = sb("slot_one_hot", [P, TOP * NT, P])
        RH = sb("block_one_hot", [P, TOP * NT, 2, NBW])
        BE = sb("block_over", [1, NBW, NE])
        tabf = sb("block_rows", [1, 4, NBW])
        tok = sb("slot_token", [P, 4, NBW])
        tri = sb("before", [P, P])
        ones = sb("ones", [P, P])
        gw = sb("group_weight", [P, n_groups])
        ew = sb("expert_weight", [P, NE])
        reset = sb("reset", [P, NE, NT])
        i128 = sb("iota_slot", [P, P])
        iblk = sb("iota_block", [P, NBW])
        ithr = sb("iota_threshold", [P, NT])
        tokp1 = sb("token_plus_1", [P, NT])
        dump = sb("dump_row", [P, 1])
        ii = sb("iota_int", [P, P], I32)
        zero = sb("zero_rows", [P, D])
        pt = [ps(f"xT{k}", [P, BANK]) for k in range(4)]
        plg = ps("logits_psum", [P, BANK])
        pcs = [ps(f"counts{k}", [P, BANK]) for k in range(2)]
        psl = ps("slots_psum", [P, BANK])

        x_in = [sem(f"x1_in{k}") for k in range(4)]
        w_in = sem("router_in")
        made = sem("iotas_made")
        t_ps = sem("x1T_in_psum")
        t_lo = sem("x1T_first_half")
        t_hi = sem("x1T_second_half")
        l_ps = sem("logits_in_psum")
        l_done = sem("logits_taken")
        centred = sem("logits_centred")
        expd = sem("exp_ready")
        m_done = sem("choices_ready")
        c_ps = sem("counts_in_psum")
        oh_done = sem("one_hots_ready")
        s_ps = sem("slots_in_psum")
        zero_out = sem("dump_rows_zeroed")
        own_sem = sem("dve_own")
        pool_sem = sem("pool_own")

        block = ctx.enter_context(nc.Block())

        @block.sync
        def _(sp):
            sp.dma_start(RW[:], router_w.rearrange("(c p) n -> p c n", p=P)).then_inc(w_in, 16)
            sp.dma_start(RB[:], router_b.partition_broadcast(P)).then_inc(w_in, 16)
            for t in range(4):
                sp.dma_start(X[:, t], x1_dram[t * P:(t + 1) * P]).then_inc(x_in[t], 16)
            with sp.Fori(1, NT // 4) as q:
                for t in range(4):
                    sp.wait_ge(t_ps, q * 4 + t - 3)
                    sp.dma_start(X[:, t], x1_dram[bass.ds(q * 4 * P + t * P, P)]).then_inc(x_in[t], 16)
            sp.wait_ge(made, 1)
            sp.dma_start(acc_dram[S:S + P], zero[:]).then_inc(zero_out, 16)
            sp.wait_ge(zero_out, 16)

        @block.gpsimd
        def _(pool):
            pool.memset(zero[:], 0.0).then_inc(made, 1)
            own = Order(pool, pool_sem, 0)

            def iota(dst, src, **how):
                if own.n:
                    own.wait()
                own.step(pool.iota(src, **how))
                own.wait()
                own.step(pool.tensor_copy(dst, src))

            iota(i128[:], ii[:], pattern=[[1, P]], base=0, channel_multiplier=0)
            iota(iblk[:], ii[:, 0:NBW], pattern=[[1, NBW]], base=0, channel_multiplier=0)
            iota(ithr[:], ii[:, 0:NT], pattern=[[P, NT]], base=0, channel_multiplier=0)
            iota(tokp1[:], ii[:, 0:NT], pattern=[[P, NT]], base=1, channel_multiplier=1)
            iota(dump[:], ii[:, 0:1], pattern=[[1, 1]], base=S + 1, channel_multiplier=1)
            iota(gw[:], ii[:, 0:n_groups], pattern=[[-1, n_groups]], base=n_groups, channel_multiplier=0)
            iota(ew[:], ii[:, 0:NE], pattern=[[-1, NE]], base=NE, channel_multiplier=0)
            own.step(pool.memset(ones[:], 1.0))
            own.step(pool.memset(reset[:], 1.0))
            own.wait()
            own.step(pool.memset(reset[:, :, 0:1], 0.0))
            own.step(pool.affine_select(out=tri[:], in_=ones[:], compare_op=ALU.is_gt, fill=0.0, base=0,
                                        pattern=[[1, P]], channel_multiplier=-1))
            own.wait()
            pool.nop().then_inc(made, 1)

        @block.scalar
        def _(act):
            with act.Fori(0, NT // 2) as q:
                for k in range(2):
                    act.wait_ge(t_ps, q * 2 + k + 1)
                    if k == 0:
                        act.wait_ge(l_ps, q * 2)
                    act.activation(XT[:, k, 0:4], pt[2 * k][:].rearrange("p (c n) -> p c n", c=4),
                                   ACT.Copy).then_inc(t_lo, 1)
            act.wait_ge(centred, 1)
            act.activation(LG[:], LG[:], ACT.Exp).then_inc(expd, 1)

        @block.tensor
        def _(pe):
            def transposes(t, k, slot):
                pe.wait_ge(t_hi, t - 1)
                pe.wait_ge(t_lo, t - 1)
                for c in range(KC):
                    ins = pe.transpose(pt[2 * k + c // 4][:, (c % 4) * P:(c % 4 + 1) * P],
                                       X[:, slot, c * P:(c + 1) * P], keep.ident[:])
                ins.then_inc(t_ps, 1)

            def logits(t, k):
                pe.wait_ge(t_lo, t + 1)
                pe.wait_ge(t_hi, t + 1)
                pe.wait_ge(l_done, t)
                for c in range(KC):
                    ins = pe.matmul(plg[:, 0:NE], XT[:, k, c], RW[:, c], start=(c == 0), stop=(c == KC - 1))
                ins.then_inc(l_ps, 1)

            pe.wait_ge(w_in, 32)
            for t in range(2):
                pe.wait_ge(x_in[t], 16)
                for c in range(KC):
                    ins = pe.transpose(pt[2 * t + c // 4][:, (c % 4) * P:(c % 4 + 1) * P],
                                       X[:, t, c * P:(c + 1) * P], keep.ident[:])
                ins.then_inc(t_ps, 1)
            logits(0, 0)
            logits(1, 1)
            for t in (2, 3):
                pe.wait_ge(x_in[t], 16)
                transposes(t, t % 2, t)
                logits(t, t % 2)
            with pe.Fori(1, NT // 4) as q:
                for t in range(4):
                    pe.wait_ge(x_in[t], (q + 1) * 16)
                    transposes(q * 4 + t, t % 2, t)
                    logits(q * 4 + t, t % 2)
            pe.wait_ge(m_done, 1)
            pe.wait_ge(made, 2)
            pe.matmul(pcs[0][:, 0:NT * NE], tri[:], E16[:, 6], start=True, stop=True)
            pe.matmul(pcs[1][:, 0:NT * NE], ones[:], E16[:, 6], start=True, stop=True).then_inc(c_ps, 1)
            pe.wait_ge(oh_done, 1)
            for n in range(TOP * NT):
                ins = pe.matmul(psl[:, 0:2 * NBW], LOH[:, n], RH[:, n].rearrange("p a b -> p (a b)"),
                                start=(n == 0), stop=(n == TOP * NT - 1))
            ins.then_inc(s_ps, 1)

        @block.vector
        def _(dve):
            own = Order(dve, own_sem, 0)

            def do(instruction):
                own.step(instruction)
                own.wait()

            dve.wait_ge(w_in, 32)
            with dve.Fori(0, NT // 2) as q:
                for k in range(2):
                    dve.wait_ge(t_ps, q * 2 + k + 1)
                    if k == 0:
                        dve.wait_ge(l_ps, q * 2)
                    dve.tensor_copy(XT[:, k, 4:8], pt[2 * k + 1][:].rearrange("p (c n) -> p c n", c=4))\
                       .then_inc(t_hi, 1)
                    dve.wait_ge(l_ps, q * 2 + k + 1)
                    dve.tensor_tensor(LG[:, bass.ds(q * (2 * NE) + k * NE, NE)], plg[:, 0:NE], RB[:], ALU.add)\
                       .then_inc(l_done, 1)
            dve.wait_ge(l_done, NT)
            dve.wait_ge(made, 2)

            def by_token(a):
                return a.rearrange("p (t e) -> p t e", t=NT)

            def spread(a, *shape):
                return a.unsqueeze(2).to_broadcast([P, *shape])

            mx, sm, gm, km, t1, t2, rs = (rows[:, k] for k in range(7))
            lg = by_token(LG[:])
            do(dve.tensor_reduce(mx, lg, AX.X, ALU.max))
            dve.tensor_tensor(lg, lg, spread(mx, NT, NE), ALU.subtract).then_inc(centred, 1)
            dve.wait_ge(expd, 1)
            do(dve.tensor_reduce(sm, lg, AX.X, ALU.add))
            do(dve.reciprocal(sm, sm))
            do(dve.tensor_tensor(lg, lg, spread(sm, NT, NE), ALU.mult))
            four = LG[:].rearrange("p (g e) -> p g e", e=PG)
            own.step(dve.tensor_tensor(HI[:], four[:, :, 0:PG:2], four[:, :, 1:PG:2], ALU.max))
            do(dve.tensor_tensor(LO[:], four[:, :, 0:PG:2], four[:, :, 1:PG:2], ALU.min))
            own.step(dve.tensor_tensor(G4[:, 0], HI[:, :, 0], HI[:, :, 1], ALU.max))
            own.step(dve.tensor_tensor(G4[:, 1], HI[:, :, 0], HI[:, :, 1], ALU.min))
            do(dve.tensor_tensor(G4[:, 2], LO[:, :, 0], LO[:, :, 1], ALU.max))
            do(dve.tensor_tensor(G4[:, 1], G4[:, 1], G4[:, 2], ALU.max))
            do(dve.tensor_tensor(G4[:, 3], G4[:, 0], G4[:, 1], ALU.add))
            gsum, gsel = (G4[:, k].rearrange("p (t g) -> p t g", t=NT) for k in (3, 4))
            do(dve.tensor_reduce(gm, gsum, AX.X, ALU.max))
            do(dve.tensor_tensor(gsel, gsum, spread(gm, NT, n_groups), ALU.is_equal))
            do(dve.tensor_tensor(gsel, gsel, gw[:].unsqueeze(1).to_broadcast([P, NT, n_groups]), ALU.mult))
            do(dve.tensor_reduce(km, gsel, AX.X, ALU.max))
            do(dve.tensor_tensor(gsel, gsel, spread(km, NT, n_groups), ALU.is_equal))
            pm, oh1, oh2, key, slot, prod, both, exc, tot = (E16[:, k] for k in range(9))
            of_group = G4[:, 4].unsqueeze(2).to_broadcast([P, NT * n_groups, PG])
            own.step(dve.tensor_tensor(pm.rearrange("p (g e) -> p g e", e=PG), four, of_group, ALU.mult))
            do(dve.tensor_scalar(G4[:, 5], G4[:, 4], -1.0, None, ALU.add))
            do(dve.tensor_tensor(pm.rearrange("p (g e) -> p g e", e=PG), pm.rearrange("p (g e) -> p g e", e=PG),
                                 G4[:, 5].unsqueeze(2).to_broadcast([P, NT * n_groups, PG]), ALU.add))
            for top, oh in ((t1, oh1), (t2, oh2)):
                do(dve.tensor_reduce(top, by_token(pm), AX.X, ALU.max))
                do(dve.tensor_tensor(by_token(key), by_token(pm), spread(top, NT, NE), ALU.is_equal))
                do(dve.tensor_tensor(by_token(key), by_token(key), ew[:].unsqueeze(1).to_broadcast([P, NT, NE]),
                                     ALU.mult))
                do(dve.tensor_reduce(km, by_token(key), AX.X, ALU.max))
                do(dve.tensor_tensor(by_token(oh), by_token(key), spread(km, NT, NE), ALU.is_equal))
                if oh is oh1:
                    do(dve.scalar_tensor_tensor(out=pm, in0=oh1, scalar=-4.0, in1=pm, op0=ALU.mult, op1=ALU.add))
            dve.tensor_tensor(both, oh1, oh2, ALU.add).then_inc(m_done, 1)
            do(dve.tensor_tensor(rs, t1, t2, ALU.add))
            do(dve.reciprocal(rs, rs))
            own.step(dve.tensor_tensor(gate[:, 0], t1, rs, ALU.mult))
            own.step(dve.tensor_tensor(gate[:, 1], t2, rs, ALU.mult))
            dve.wait_ge(c_ps, 1)
            et = "p (e t) -> p e t"
            do(dve.tensor_copy(tot.rearrange(et, e=NE), pcs[1][:, 0:NT * NE].rearrange("p (t e) -> p e t", t=NT)))
            do(dve.tensor_tensor_scan(exc, reset[:].rearrange("p e t -> p (e t)"), tot, 0.0, ALU.mult, ALU.add))
            count, blocks, end, start = (cnt[:, k] for k in range(4))
            do(dve.tensor_copy(count, exc.rearrange(et, e=NE)[:, :, NT - 1]))
            own.step(dve.tensor_tensor(thr[:], spread(count, NE, NT), ithr[:].unsqueeze(1).to_broadcast([P, NE, NT]),
                                       ALU.is_gt))
            do(dve.tensor_tensor(exc, exc, tot, ALU.subtract))
            do(dve.tensor_reduce(blocks, thr[:], AX.X, ALU.add))
            do(dve.tensor_tensor_scan(end, ones[:, 0:NE], blocks, 0.0, ALU.mult, ALU.add))
            do(dve.tensor_tensor(start, end, blocks, ALU.subtract))
            do(dve.tensor_scalar(start, start, float(P), None, ALU.mult))
            do(dve.tensor_tensor(exc.rearrange(et, e=NE), exc.rearrange(et, e=NE), spread(start, NE, NT), ALU.add))
            do(dve.tensor_tensor(by_token(slot), pcs[0][:, 0:NT * NE].rearrange("p (t e) -> p t e", t=NT),
                                 exc.rearrange("p (e t) -> p t e", e=NE), ALU.add))
            for k, oh in enumerate((oh1, oh2)):
                do(dve.tensor_tensor(prod, oh, slot, ALU.mult))
                do(dve.tensor_reduce(rows[:, 8 + k], by_token(prod), AX.X, ALU.add))
            do(dve.tensor_copy(slot_i[:, 0], rows[:, 8:10].rearrange("p a b -> p (a b)")))
            own.step(dve.tensor_scalar(slot_i[:, 1], slot_i[:, 0], 7, None, ALU.arith_shift_right))
            do(dve.tensor_scalar(slot_i[:, 2], slot_i[:, 0], P - 1, None, ALU.bitwise_and))
            do(dve.tensor_copy(slot_f[:], slot_i[:, 1:3]))
            N = TOP * NT
            own.step(dve.tensor_tensor(LOH[:], i128[:].unsqueeze(1).to_broadcast([P, N, P]),
                                       slot_f[:, 1].unsqueeze(2).to_broadcast([P, N, P]), ALU.is_equal))
            do(dve.tensor_tensor(RH[:, :, 1], iblk[:].unsqueeze(1).to_broadcast([P, N, NBW]),
                                 slot_f[:, 0].unsqueeze(2).to_broadcast([P, N, NBW]), ALU.is_equal))
            for k in range(TOP):
                own.step(dve.tensor_tensor(RH[:, k * NT:(k + 1) * NT, 0], RH[:, k * NT:(k + 1) * NT, 1],
                                           tokp1[:].unsqueeze(2).to_broadcast([P, NT, NBW]), ALU.mult))
            own.wait()
            own.step(dve.tensor_tensor(RH[:, :, 1], RH[:, :, 1],
                                       gate[:].rearrange("p a b -> p (a b)").unsqueeze(2).to_broadcast([P, N, NBW]),
                                       ALU.mult))
            own.wait()
            dve.sem_inc(oh_done, 1)
            be, fresh, before, earlier = (tabf[:, k] for k in range(4))
            do(dve.tensor_tensor(BE[:], end[0:1].unsqueeze(1).to_broadcast([1, NBW, NE]),
                                 iblk[0:1].unsqueeze(2).to_broadcast([1, NBW, NE]), ALU.is_le))
            do(dve.tensor_reduce(be, BE[:], AX.X, ALU.add))
            do(dve.tensor_scalar(be, be, float(NE - 1), None, ALU.min))
            own.step(dve.memset(fresh[:, 0:1], 1.0))
            own.step(dve.memset(fresh[:, NBW - 1:], 0.0))
            do(dve.tensor_tensor(fresh[:, 1:NBW - 1], be[:, 1:NBW - 1], be[:, 0:NBW - 2], ALU.not_equal))
            do(dve.tensor_tensor_scan(before, ones[0:1, 0:NBW], fresh, -1.0, ALU.mult, ALU.add))
            do(dve.tensor_scalar(earlier, before, -1.0, 0.0, ALU.add, ALU.max))
            own.step(dve.tensor_copy(keep.table[:], tabf[:]))
            dve.wait_ge(s_ps, 1)
            own.step(dve.tensor_copy(tok[:, 0], psl[:, 0:NBW]))
            do(dve.tensor_copy(keep.gate[:], psl[:, NBW:2 * NBW]))
            own.step(dve.tensor_scalar(tok[:, 1], tok[:, 0], -1.0, 0.0, ALU.add, ALU.max))
            own.step(dve.tensor_scalar(tok[:, 2], tok[:, 0], 0.0, None, ALU.is_equal))
            do(dve.tensor_scalar(tok[:, 3], tok[:, 0], -1.0, None, ALU.add))
            do(dve.scalar_tensor_tensor(out=tok[:, 3], in0=tok[:, 2], scalar=dump[:, 0:1], in1=tok[:, 3],
                                        op0=ALU.mult, op1=ALU.add))
            dve.tensor_copy(keep.gather[:], tok[:, 1])
            do(dve.tensor_copy(keep.scatter[:], tok[:, 3]))


def experts(nc, keep, x1_dram, acc_dram, w_gate, w_up, w_down):
    D = x1_dram.shape[1]
    NE, _, F = w_gate.shape
    KC = D // P
    FC = F // P
    NBLK = keep.gather.shape[1] - 1
    NGU, NDN = KC // 2, FC // 2
    NPAIR = NGU + NDN
    assert F == BANK and D == 2 * BANK and NBLK % 2 == 1

    ctx = ExitStack()
    with ctx:
        sb, ps, sem = tensors(nc, ctx, "moe")
        raw = sb("w_raw", [P, NPAIR, 2, D])
        wh, wl = (sb(n, [P, NPAIR, 2, D], F32R) for n in ("w_high", "w_low"))
        X = sb("x_rows", [P, 2, D])
        xTh, xTl = (sb(n, [P, 2, KC, P], F32R) for n in ("xT_high", "xT_low"))
        sig = sb("sigmoid", [P, F])
        hid = sb("hidden", [P, F])
        hTh, hTl = (sb(n, [P, FC, P], F32R) for n in ("hiddenT_high", "hiddenT_low"))
        Y = sb("y_rows", [P, 2, D])
        gi, si = (sb(n, [P, 2], I32) for n in ("gather_index", "scatter_index"))
        pg, pu = ps("gate_psum", [P, BANK]), ps("up_psum", [P, BANK])
        py = [ps(f"y_psum{k}", [P, BANK]) for k in range(2)]
        px = [ps(f"xT_psum{k}", [P, BANK]) for k in range(2)]
        ph = ps("hiddenT_psum", [P, BANK])

        raw_in = [sem(f"w_raw_in{k}") for k in range(3)]
        gu_h, gu_l = sem("gate_up_high_ready"), sem("gate_up_low_ready")
        dn_h, dn_l = sem("down_high_ready"), sem("down_low_ready")
        gu_used, dn_used = sem("gate_up_used"), sem("down_used")
        x_in = [sem(f"x_rows_in{k}") for k in range(2)]
        x_ps, xh_done, xl_done = sem("xT_in_psum"), sem("xT_high_ready"), sem("xT_low_ready")
        sig_done, hid_done = sem("sigmoid_ready"), sem("hidden_ready")
        ht_ps, hh_done, hl_done = sem("hiddenT_in_psum"), sem("hiddenT_high_ready"), sem("hiddenT_low_ready")
        y_act, y_dve = sem("y_first_half"), sem("y_second_half")
        added, y_free = sem("y_added"), sem("y_slot_free")
        dve_own, pool_own, pool_idle = sem("dve_own"), sem("pool_own"), sem("pool_wait_carrier")

        def entry(engine, row, b):
            return engine.value_load(keep.table[0:1, row, bass.ds(b, 1)], min_val=0, max_val=(NE - 1, 1, NE, NE)[row])

        block = ctx.enter_context(nc.Block())

        @block.sync
        def _(sp):
            def load(e, n, before, first):
                half = KC // 2
                for part in range(3):
                    if not first:
                        if part < 2:
                            sp.wait_ge(gu_l, before * NGU + (part + 1) * 2)
                        else:
                            sp.wait_ge(dn_l, n * NDN)
                    if part < 2:
                        dst = raw[:, 2 * part:2 * part + 2].rearrange("p a c n -> p (a c) n")
                        for k, w in enumerate((w_gate, w_up)):
                            src = w[bass.ds(e, 1), part * half * P:(part + 1) * half * P, :]
                            sp.dma_start(dst[:, :, k * F:(k + 1) * F], src.rearrange("a (c p) n -> p (a c) n", p=P))\
                              .then_inc(raw_in[part], 16)
                    else:
                        for k in range(NDN):
                            src = w_down[bass.ds(e, 1), 2 * k * P:2 * (k + 1) * P, :]
                            sp.dma_start(raw[:, NGU + k], src.rearrange("a (c p) n -> p (a c) n", p=P))\
                              .then_inc(raw_in[part], 16)

            load(entry(sp, 0, 0), 0, 0, True)
            with sp.Fori(1, NBLK) as b:
                fresh = entry(sp, 1, b)
                with sp.If(fresh):
                    load(entry(sp, 0, b), entry(sp, 2, b), entry(sp, 3, b), False)

        @block.gpsimd
        def _(pool):
            POOL_TURN = 4
            own = Order(pool, pool_own, POOL_TURN, 2)

            def gather(b, k):
                pool.indirect_dma_start(out=X[:, k], out_offset=None, in_=x1_dram,
                                        in_offset=bass.IndirectOffsetOnAxis(ap=gi[:, k:k + 1], axis=0))\
                    .then_inc(x_in[k], 16)

            def scatter(k):
                pool.indirect_dma_start(out=acc_dram, out_offset=bass.IndirectOffsetOnAxis(ap=si[:, k:k + 1], axis=0),
                                        in_=Y[:, k], in_offset=None, compute_op=ALU.add).then_inc(added, 16)

            for k in range(2):
                pool.tensor_copy(gi[:, k:k + 1], keep.gather[:, k:k + 1]).then_inc(pool_own, 1)
            pool.wait_ge(pool_own, 2)
            for k in range(2):
                gather(k, k)
            with pool.Fori(0, NBLK // 2) as j:
                for i in range(2):
                    b = 2 * j + 1 + i
                    k = (1 + i) % 2
                    pool.wait_ge(x_ps, b)
                    own.step(pool.tensor_copy(gi[:, 1 - k:2 - k], keep.gather[:, bass.ds(b + 1, 1)]))
                    wait_apart(pool, pool_idle, *own.due(j))
                    gather(b + 1, 1 - k)
                    wait_apart(pool, y_free, added, (b - 1) * 16)
                    own.step(pool.tensor_copy(si[:, 1 - k:2 - k], keep.scatter[:, bass.ds(b - 1, 1)]))
                    pool.wait_ge(y_act, b)
                    pool.wait_ge(y_dve, b)
                    wait_apart(pool, pool_idle, *own.due(j))
                    scatter(1 - k)
            last = NBLK - 1
            pool.wait_ge(added, last * 16)
            pool.tensor_copy(si[:, 0:1], keep.scatter[:, last:last + 1]).then_inc(pool_own, 1)
            pool.wait_ge(pool_own, 2 + POOL_TURN * (NBLK // 2) + 1)
            pool.wait_ge(y_act, NBLK)
            pool.wait_ge(y_dve, NBLK)
            scatter(0)
            pool.wait_ge(added, NBLK * 16)
            assert own.n == POOL_TURN

        @block.scalar
        def _(act):
            def x_high(b, k):
                act.wait_ge(x_ps, b + 1)
                for c in range(2):
                    ins = act.activation(xTh[:, k, 4 * c:4 * c + 4], px[c][:].rearrange("p (c n) -> p c n", c=4),
                                         ACT.Copy)
                ins.then_inc(xh_done, 1)

            def split(b, n, pairs, free):
                for u in pairs:
                    gu = u < NGU
                    act.wait_ge(raw_in[u // 2], (n + 1) * 32)
                    if free:
                        if gu:
                            act.wait_ge(gu_used, (b - 1) * NGU + u + 1)
                        else:
                            act.wait_ge(dn_used, (b - 1) * NDN + u - NGU + 1)
                    act.activation(wh[:, u], raw[:, u], ACT.Copy).then_inc(gu_h if gu else dn_h, 1)

            def hidden(b):
                act.wait_ge(gu_used, (b + 1) * NGU)
                if not isinstance(b, int):
                    act.wait_ge(hid_done, b)
                act.activation(sig[:], pg[:], ACT.Sigmoid).then_inc(sig_done, 1)

            def y_half(b, k):
                act.wait_ge(dn_used, (b + 1) * NDN)
                act.wait_ge(y_free, b)
                act.activation(Y[:, k, 0:BANK], py[0][:], ACT.Copy,
                               scale=keep.gate[:, bass.ds(b, 1)]).then_inc(y_act, 1)

            def hT_high(b):
                act.wait_ge(ht_ps, b + 1)
                act.activation(hTh[:], ph[:].rearrange("p (c n) -> p c n", c=FC), ACT.Copy).then_inc(hh_done, 1)

            split(0, 0, range(NGU), False)
            x_high(0, 0)
            split(0, 0, range(NGU, NPAIR), False)
            x_high(1, 1)
            first, n = entry(act, 1, 1), entry(act, 2, 1)
            with act.If(first):
                split(1, n, range(0, NGU), True)
            hidden(0)
            hT_high(0)
            with act.Fori(0, NBLK // 2) as j:
                for i in range(2):
                    b = 2 * j + 1 + i
                    k = (1 + i) % 2
                    x_high(b + 1, 1 - k)
                    first, n = entry(act, 1, b + 1), entry(act, 2, b + 1)
                    with act.If(first):
                        split(b + 1, n, range(0, 2), True)
                    hidden(b)
                    with act.If(first):
                        split(b + 1, n, range(2, NGU), True)
                    y_half(b - 1, 1 - k)
                    hT_high(b)
                    first, n = entry(act, 1, b), entry(act, 2, b)
                    with act.If(first):
                        split(b, n, range(NGU, NPAIR), True)
            y_half(NBLK - 1, 0)

        @block.vector
        def _(dve):
            DVE_TURN = 2
            own = Order(dve, dve_own, DVE_TURN, 1)

            def x_low(b, k):
                dve.wait_ge(xh_done, b + 1)
                for c in range(2):
                    sl = (slice(None), k, slice(4 * c, 4 * c + 4))
                    ins = dve.tensor_tensor(xTl[sl], px[c][:].rearrange("p (c n) -> p c n", c=4),
                                            xTh[sl].bitcast(F32), ALU.subtract)
                ins.then_inc(xl_done, 1)

            def split(n, pairs):
                for u in pairs:
                    gu = u < NGU
                    if gu:
                        dve.wait_ge(gu_h, n * NGU + u + 1)
                    else:
                        dve.wait_ge(dn_h, n * NDN + u - NGU + 1)
                    dve.tensor_tensor(wl[:, u], raw[:, u], wh[:, u].bitcast(F32), ALU.subtract)\
                       .then_inc(gu_l if gu else dn_l, 1)

            def hidden(b, turn):
                dve.wait_ge(sig_done, b + 1)
                if not isinstance(b, int):
                    dve.wait_ge(ht_ps, b)
                ins = dve.tensor_tensor(hid[:], pg[:], sig[:], ALU.mult)
                if turn is None:
                    ins.then_inc(dve_own, 1)
                    dve.wait_ge(dve_own, 1)
                else:
                    own.step(ins)
                    own.wait(turn)
                dve.tensor_tensor(hid[:], hid[:], pu[:], ALU.mult).then_inc(hid_done, 1)

            def y_half(b, k):
                dve.wait_ge(dn_used, (b + 1) * NDN)
                dve.wait_ge(y_free, b)
                dve.tensor_scalar(Y[:, k, BANK:], py[1][:], keep.gate[:, bass.ds(b, 1)], None,
                                  ALU.mult).then_inc(y_dve, 1)

            def hT_low(b):
                dve.wait_ge(hh_done, b + 1)
                dve.tensor_tensor(hTl[:], ph[:].rearrange("p (c n) -> p c n", c=FC), hTh[:].bitcast(F32),
                                  ALU.subtract).then_inc(hl_done, 1)

            split(0, range(NGU))
            x_low(0, 0)
            split(0, range(NGU, NPAIR))
            x_low(1, 1)
            first, n = entry(dve, 1, 1), entry(dve, 2, 1)
            with dve.If(first):
                split(n, range(0, NGU))
            hidden(0, None)
            hT_low(0)
            with dve.Fori(0, NBLK // 2) as j:
                for i in range(2):
                    b = 2 * j + 1 + i
                    k = (1 + i) % 2
                    x_low(b + 1, 1 - k)
                    first, n = entry(dve, 1, b + 1), entry(dve, 2, b + 1)
                    with dve.If(first):
                        split(n, range(0, 2))
                    hidden(b, j)
                    with dve.If(first):
                        split(n, range(2, NGU))
                    y_half(b - 1, 1 - k)
                    hT_low(b)
                    first, n = entry(dve, 1, b), entry(dve, 2, b)
                    with dve.If(first):
                        split(n, range(NGU, NPAIR))
            y_half(NBLK - 1, 0)
            assert own.n == DVE_TURN

        @block.tensor
        def _(pe):
            def three(out, ah, al, bh, bl, first, last):
                pe.matmul(out, ah, bh, start=first, stop=False)
                pe.matmul(out, ah, bl, start=False, stop=False)
                return pe.matmul(out, al, bh, start=False, stop=last)

            def turn_x(b, k, use):
                pe.wait_ge(x_in[k], (use + 1) * 16)
                if not isinstance(b, int) or b:
                    pe.wait_ge(xl_done, b)
                for c in range(KC):
                    ins = pe.transpose(px[c // 4][:, (c % 4) * P:(c % 4 + 1) * P], X[:, k, c * P:(c + 1) * P],
                                       keep.ident[:])
                ins.then_inc(x_ps, 1)

            def gate_up(b, k, n):
                pe.wait_ge(xl_done, b + 1)
                if not isinstance(b, int):
                    pe.wait_ge(hid_done, b)
                for u in range(NGU):
                    pe.wait_ge(gu_l, n * NGU + u + 1)
                    for c in range(2):
                        kc = 2 * u + c
                        for out, s in ((pg, slice(0, F)), (pu, slice(F, 2 * F))):
                            ins = three(out[:], xTh[:, k, kc], xTl[:, k, kc], wh[:, u, c, s], wl[:, u, c, s],
                                        kc == 0, kc == KC - 1)
                    ins.then_inc(gu_used, 1)

            def down(b, n):
                pe.wait_ge(hl_done, b + 1)
                if not isinstance(b, int) or b:
                    pe.wait_ge(y_act, b)
                    pe.wait_ge(y_dve, b)
                for u in range(NDN):
                    pe.wait_ge(dn_l, n * NDN + u + 1)
                    for c in range(2):
                        kc = 2 * u + c
                        for q in range(2):
                            s = slice(q * BANK, (q + 1) * BANK)
                            ins = three(py[q][:], hTh[:, kc], hTl[:, kc], wh[:, NGU + u, c, s], wl[:, NGU + u, c, s],
                                        kc == 0, kc == FC - 1)
                    ins.then_inc(dn_used, 1)

            def turn_hidden(b):
                pe.wait_ge(hid_done, b + 1)
                if not isinstance(b, int):
                    pe.wait_ge(hl_done, b)
                for c in range(FC):
                    ins = pe.transpose(ph[:, c * P:(c + 1) * P], hid[:, c * P:(c + 1) * P], keep.ident[:])
                ins.then_inc(ht_ps, 1)

            turn_x(0, 0, 0)
            turn_x(1, 1, 0)
            gate_up(0, 0, 0)
            turn_hidden(0)
            with pe.Fori(0, NBLK // 2) as j:
                for i in range(2):
                    b = 2 * j + 1 + i
                    k = (1 + i) % 2
                    turn_x(b + 1, 1 - k, j + 1)
                    gate_up(b, k, entry(pe, 2, b))
                    down(b - 1, entry(pe, 2, b - 1))
                    turn_hidden(b)
            down(NBLK - 1, entry(pe, 2, NBLK - 1))


def final_norm(nc, acc_dram, ln_g, ln_b, out):
    S, D = out.shape
    NT = S // P
    SL = 4

    ctx = ExitStack()
    with ctx:
        sb, ps, sem = tensors(nc, ctx, "norm")
        R = sb("rows", [P, SL, D])
        O = sb("normed", [P, SL, D])
        lng, lnb = (sb(n, [P, D]) for n in ("ln_gain", "ln_bias"))
        stats = sb("stats", [P, SL, 2, 6])
        mv = sb("mean_var", [P, SL, 2])
        rstd = sb("rstd", [P, SL])
        shift = sb("shift", [P, SL])
        eps = sb("eps", [P, 1])
        r_in = [sem(f"rows_in{k}") for k in range(SL)]
        ln_in = sem("ln_in")
        var_done, rs_done, sh_done = sem("var_ready"), sem("rstd_ready"), sem("shift_ready")
        n_done, o_done = sem("normed_ready"), sem("scaled_ready")
        stored = [sem(f"out_stored{k}") for k in range(SL)]
        dve_own, act_own, dve_idle, pool_own = (sem("dve_own"), sem("act_own"), sem("dve_wait_carrier"),
                                                sem("pool_own"))
        block = ctx.enter_context(nc.Block())

        @block.sync
        def _(sp):
            for v, dst in ((ln_g, lng), (ln_b, lnb)):
                sp.dma_start(dst[:], v.partition_broadcast(P)).then_inc(ln_in, 16)
            for k in range(SL):
                sp.dma_start(R[:, k], acc_dram[k * P:(k + 1) * P]).then_inc(r_in[k], 16)
            with sp.Fori(1, NT // SL) as q:
                for k in range(SL):
                    sp.wait_ge(n_done, q * SL + k - SL + 1)
                    sp.dma_start(R[:, k], acc_dram[bass.ds(q * (SL * P) + k * P, P)]).then_inc(r_in[k], 16)

        @block.scalar
        def _(act):
            act.wait_ge(ln_in, 32)
            with act.Fori(0, NT // SL) as q:
                for k in range(SL):
                    t = q * SL + k
                    act.wait_ge(var_done, t + 1)
                    act.activation(rstd[:, k:k + 1], mv[:, k, 1:2], ACT.Sqrt, bias=eps[:, 0:1]).then_inc(rs_done, 1)
                    act.wait_ge(sh_done, t + 1)
                    act.wait_ge(stored[k], q * 16)
                    act.activation(O[:, k], R[:, k], ACT.Identity, bias=shift[:, k:k + 1],
                                   scale=rstd[:, k:k + 1]).then_inc(n_done, 1)
                    act.wait_ge(o_done, t + 1)
                    act.dma_start(out[bass.ds(q * (SL * P) + k * P, P)], O[:, k]).then_inc(stored[k], 16)
            for k in range(SL):
                act.wait_ge(stored[k], NT // SL * 16)

        @block.vector
        def _(dve):
            TURN = 3 * SL
            own = Order(dve, dve_own, TURN)
            dve.memset(eps[:], LN_EPS)
            dve.wait_ge(ln_in, 32)
            with dve.Fori(0, NT // SL) as q:
                for k in range(SL):
                    t = q * SL + k
                    dve.wait_ge(r_in[k], (q + 1) * 16)
                    for h in range(2):
                        ins = dve.bn_stats(stats[:, k, h], R[:, k, h * BANK:(h + 1) * BANK])
                    own.step(ins)
                    wait_apart(dve, dve_idle, *own.due(q))
                    dve.bn_aggr(mv[:, k], stats[:, k]).then_inc(var_done, 1)
                    dve.wait_ge(rs_done, t + 1)
                    own.step(dve.reciprocal(rstd[:, k:k + 1], rstd[:, k:k + 1]))
                    own.wait(q)
                    dve.scalar_tensor_tensor(out=shift[:, k:k + 1], in0=mv[:, k, 0:1], scalar=-1.0,
                                             in1=rstd[:, k:k + 1], op0=ALU.mult, op1=ALU.mult).then_inc(sh_done, 1)
                    dve.wait_ge(n_done, t + 1)
                    own.step(dve.tensor_tensor(O[:, k], O[:, k], lng[:], ALU.mult))
                    own.wait(q)
                    dve.tensor_tensor(O[:, k], O[:, k], lnb[:], ALU.add).then_inc(o_done, 1)
            assert own.n == TURN


class Kept:
    pass


def hybrid_layer(nc, x, w_in, b_in, conv_w, mh_g, w_out, ln_mix_g, ln_mix_b, router_w, router_b,
                 w_gate, w_up, w_down, ln_moe_g, ln_moe_b, out, alpha, n_groups):
    S, D = x.shape
    NE = router_w.shape[1]
    most = (2 * S + NE * (P - 1)) // P
    x1_dram = nc.dram_tensor("x1", [S, D], F32, kind="Internal").ap()
    acc_dram = nc.dram_tensor("gathered", [S + P, D], F32, kind="Internal").ap()
    ctx = ExitStack()
    with ctx:
        sb, ps, sem = tensors(nc, ctx, "kept")
        keep = Kept()
        keep.ident = sb("identity", [P, P])
        keep.gather = sb("slot_gather_row", [P, most + 1], I32)
        keep.scatter = sb("slot_scatter_row", [P, most + 1], I32)
        keep.gate = sb("slot_gate", [P, most + 1])
        keep.table = sb("block_table", [1, 4, most + 1], I32)
        mixer(nc, keep, x, w_in, b_in, conv_w, mh_g, w_out, ln_mix_g, ln_mix_b, x1_dram, acc_dram, alpha)
        route(nc, keep, x1_dram, acc_dram, router_w, router_b, n_groups)
        experts(nc, keep, x1_dram, acc_dram, w_gate, w_up, w_down)
        final_norm(nc, acc_dram, ln_moe_g, ln_moe_b, out)


_STACKED = ("w_in", "b_in", "conv_w", "mh_norm_g", "w_out", "ln_mix_g", "ln_mix_b")
_SHARED = ("router_w", "router_b")
_EXPERT = ("w_gate", "w_up", "w_down", "ln_moe_g", "ln_moe_b")
N_EXPERT_GROUPS = 4


def kernel(**inputs):
    import numpy as _np
    import concourse.bacc as _bacc
    from concourse import mybir as _mybir
    from concourse.bass_utils import run_bass_kernel_spmd as _run

    nc = _bacc.Bacc("TRN2", target_bir_lowering=False, num_devices=1)
    x = _np.asarray(inputs["x"])
    depth = inputs["w_in"].shape[0]
    assert x.shape[0] == 1 and depth == 1
    arrays, args = {}, []
    for name in ("x",) + _STACKED + _SHARED + _EXPERT:
        a = _np.asarray(inputs[name])
        if name not in _SHARED:
            a = a[0]
        a = _np.ascontiguousarray(a)
        arrays[f"in_{name}"] = a
        args.append(nc.dram_tensor(f"in_{name}", a.shape, _mybir.dt.from_np(a.dtype), kind="ExternalInput").ap())
    out = nc.dram_tensor("out_x", x.shape[1:], _mybir.dt.from_np(x.dtype), kind="ExternalOutput").ap()
    hybrid_layer(nc, *args, out, alpha=(2 * depth) ** 0.25, n_groups=N_EXPERT_GROUPS)
    r = _run(nc, [arrays], core_ids=[0])
    return _np.asarray(r.results[0]["out_x"]).reshape(x.shape)
```

```python
import concourse.bass as bass
from concourse import mybir
from contextlib import ExitStack

P = 128
F32 = mybir.dt.float32
F32R = mybir.dt.float32r
BF16 = mybir.dt.bfloat16
I32 = mybir.dt.int32
ALU = mybir.AluOpType
ACT = mybir.ActivationFunctionType
AX_ = mybir.AxisListType

LN_EPS = 1e-5
BANK = 512
MASKED = -1e30
LOWEST = -3e38
EXP_AND_LN = 6


def tensors(nc, ctx, stage):
    def sb(name, shape, dt=F32):
        return ctx.enter_context(nc.sbuf_tensor(f"{stage}_{name}", shape, dt))

    def ps(name, shape, dt=F32):
        return ctx.enter_context(nc.psum_tensor(f"{stage}_{name}", shape, dt))

    def sem(name):
        return ctx.enter_context(nc.semaphore(f"{stage}_{name}"))

    return sb, ps, sem


def wait_apart(engine, carrier, sem, value):
    engine.wait_ge(sem, value)
    engine.sem_inc(carrier, 1)


class Order:

    def __init__(self, engine, sem, per_turn, before=0):
        self.engine, self.sem, self.per_turn, self.before, self.n = engine, sem, per_turn, before, 0

    def step(self, instruction):
        self.n += 1
        instruction.then_inc(self.sem, 1)

    def due(self, turn=0):
        return self.sem, turn * self.per_turn + self.before + self.n

    def wait(self, turn=0):
        self.engine.wait_ge(*self.due(turn))


def mixer(nc, keep, x, w_in, b_in, conv_w, mh_g, w_out, ln_g, ln_b, x1_dram, acc_dram, alpha):
    S, D = x.shape
    DM = w_out.shape[0] // 2
    NH = 4
    DH = DM // NH
    TAPS = conv_w.shape[0]
    GT = BANK
    NG = S // GT
    NT = GT // P
    KC = D // P
    KH = KC // 2
    OFF_I = 4 * DM
    OFF_F = OFF_I + NH
    OFF_B = OFF_F + NH
    OFF_C = OFF_B + DM
    OFF_X = OFF_C + DM
    QB, KB, VB, OB, CB, XB, BB, OUT0, OUT1 = range(9)
    BLOCK_COL = {QB: 0, KB: DM, VB: 2 * DM, OB: 3 * DM, CB: OFF_C, XB: OFF_X, BB: OFF_B, OUT0: 0, OUT1: BANK}
    BY_CHANNEL = (QB, KB, CB, XB, BB)
    BY_ACT = (QB, CB)
    NB = 9
    ST = 2 * NB
    FULL = NB * NT
    N_ACT = len(BY_ACT) * NT
    N_DVE = FULL - N_ACT
    assert DH == P and D == 2 * BANK and DM == BANK and NT == NH and TAPS == 3
    W = DH + 1

    SLOT = {}
    for c in range(NT):
        for k in range(3):
            n = 3 * c + k
            SLOT[(8 + n // 2, 2 * (n % 2))] = ("S1", "S2", "S3")[k], c
    LAST_Y = 14
    SLOT[(LAST_Y, 0)] = "Y", NT - 1
    for t in range(NT):
        SLOT[(15 + t // 2, 2 * (t % 2))] = "X", t

    SIGMOID_STAGE = (8, 9, 11, 12)
    Y_CONV = 2 * BB + 1

    def previous(b):
        return (b - 1) % NB

    def dve_count(b):
        return sum(1 for k in range(b) if k not in BY_ACT)

    def act_count(b):
        return sum(1 for k in range(b) if k in BY_ACT)

    ctx = ExitStack()
    with ctx:
        sb, ps, sem = tensors(nc, ctx, "mix")
        xTh, xTl = (sb(n, [P, KC, GT], F32R) for n in ("xT_high", "xT_low"))
        yTh, yTl = (sb(n, [P, KC, GT], F32R) for n in ("yT_high", "yT_low"))
        raw = sb("w_raw", [P, 2, KH, BANK])
        wh, wl = (sb(n, [P, 2, KH, BANK], F32R) for n in ("w_high", "w_low"))
        wgr = sb("w_gates_raw", [P, KC, 2 * NH])
        GC = 32 + NH
        wgh, wgl = (sb(n, [P, (KC - 1) * GC + P], F32R) for n in ("w_gates_high", "w_gates_low"))
        gates_h, gates_l = (w[:, 0:KC * GC].rearrange("p (c n) -> p c n", c=KC) for w in (wgh, wgl))
        qT = sb("qT", [P, NH, GT])
        kT = sb("kT", [P, NH, GT])
        V = sb("values", [P, NT, NH, W])
        OG = sb("o_gate", [P, NT, DM])
        CUR = keep.conv_or_residual
        CT = CUR[:, 0:NT * GT].rearrange("p (t n) -> p t n", t=NT)
        U = CUR[:, NT * GT:].rearrange("p (t n) -> p t n", t=NT)
        R = CUR[:, 0:NT * D].rearrange("p (t n) -> p t n", t=NT)
        lnb = keep.ln_bias
        halo = sb("u_halo", [P, NT, 2])
        XN = sb("x_rows", [P, 2, D])
        IG, FF, BR, CM = (sb(n, [NH, GT]) for n in ("row_i", "row_f", "row_b", "row_max"))
        MS = sb("row_m", [NH, NT + 1])
        GM = sb("row_g", [NH, NT])
        SPR = sb("row_decay", [NH, NT])
        ROWS = sb("rows", [P, GT])
        NAT = sb("columns", [P, NT, 4, NH])
        SPB = sb("decay", [P, NH, NT])
        DT = sb("decayed_scores", [P, NH, P])
        KE = sb("k_weighted", [P, NH, DH])
        YC = [a[:].rearrange("p h n -> p (h n)") for a in (DT, KE)]
        NU = sb("numerator", [P, NH, W])
        CS = sb("state", [P, NH, W])
        den = sb("denominator", [P, NH])
        stat = sb("head_stats", [P, NH, 6])
        mv = sb("head_mean_var", [P, NH, 2])
        rstd = sb("head_rstd", [P, NH])
        lstat = sb("ln_stats", [P, NT, 2, 6])
        lmv = sb("ln_mean_var", [P, NT, 2])
        lrs = sb("ln_rstd", [P, NT])
        ident = keep.ident
        identb = sb("ident_bf16", [P, P], BF16)
        mask = sb("causal_mask", [P, P], BF16)
        sel = sb("head_select", [NH, NH, P])
        zrow = sb("zero_row", [NH, P])
        bq, bk, bc_, bx, bb = (sb(n, [P, NT]) for n in ("b_q", "b_k", "b_c", "b_x", "b_b"))
        bi, bf = (sb(n, [NH, 1]) for n in ("b_i", "b_f"))
        eps = sb("eps", [P, 1])
        cw = sb("conv_taps", [P, TAPS, NT])
        bv, bo = (sb(n, [P, DM]) for n in ("b_v", "b_o"))
        mhg = sb("mh_gain", [P, NH])
        lng = sb("ln_gain", [P, D])

        acc = [ps(f"acc{t}", [P, BANK]) for t in range(NT)]
        aux = [ps(f"aux{t}", [P, BANK]) for t in range(4)]

        consts_in = sem("consts_in")
        gates_w_in = sem("gates_w_in")
        consts_made = sem("consts_made")
        dve_consts = sem("dve_consts")
        gates_w_split = sem("gates_w_split")
        raw_in = [sem(f"w_raw_in{k}") for k in range(2)]
        split_h = sem("w_high_ready")
        split_l = sem("w_low_ready")
        stage_used = sem("stage_used")
        x_in = [sem(f"x_rows_in{k}") for k in range(2)]
        xt_ps = sem("xT_in_psum")
        xt_h = sem("xT_high_ready")
        xt_done = sem("xT_ready")
        acc_full = sem("acc_full")
        act_out = sem("acc_taken_by_act")
        dve_out = sem("acc_taken_by_dve")
        gates_ps = sem("gates_in_psum")
        f_neg = sem("f_neg_ready")
        f_log = sem("f_log_ready")
        exps_in = sem("row_exponents_ready")
        rows_done = sem("rows_ready")
        nat_ps = sem("columns_in_psum")
        nat_done = sem("columns_ready")
        o_gate = sem("o_gate_ready")
        s1_ps = sem("scores_in_psum")
        dt_done = sem("decay_matrix_ready")
        pt_done = sem("weights_ready")
        num_ps = sem("numerators_in_psum")
        inter_done = sem("state_part_taken")
        num_done = sem("numerators_taken")
        var_done = sem("head_var_ready")
        rs_done = sem("head_rstd_ready")
        y_done = sem("y_ready")
        cl_ps = sem("chunk_state_in_psum")
        state_done = sem("state_updated")
        y_ps = sem("yT_in_psum")
        yh_done = sem("yT_high_ready")
        yl_done = sem("yT_low_ready")
        ych_done = sem("y_conv_high_ready")
        conv_done = sem("conv_group_done")
        first_x = [sem(f"first_rows_in{t}") for t in range(NT)]
        res_in = [sem(f"residual_in{t}") for t in range(NT)]
        lvar_done = sem("ln_var_ready")
        ln_gained = sem("ln_gain_applied")
        ln_done = sem("ln_normalised")
        x1_out, xa_out = sem("x1_stored"), sem("alpha_x1_stored")
        dve_own = sem("dve_own")
        act_own = sem("act_own")
        pool_own = sem("pool_own")
        pool_idle = sem("pool_wait_carrier")
        dve_idle = sem("dve_wait_carrier")

        N_CONSTS = (6 + TAPS + 2 + 4) * 16

        def w_view(stage):
            b, half = stage // 2, stage % 2
            src = w_out if b >= OUT0 else w_in
            col = BLOCK_COL[b]
            return src[half * KH * P:(half + 1) * KH * P, col:col + BANK].rearrange("(c p) n -> p c n", p=P)

        def column(v):
            return v.rearrange("(t p) -> p t", p=P)

        block = ctx.enter_context(nc.Block())

        @block.sync
        def _(sp):
            def load_stage(g, stage, after):
                n = g * ST + stage + after * ST
                if after or stage:
                    sp.wait_ge(split_l, n - 1)
                sp.dma_start(raw[:, stage % 2], w_view(stage)).then_inc(raw_in[stage % 2], 16)

            for t in range(NT):
                sp.dma_start(R[:, t], x[t * P:(t + 1) * P]).then_inc(first_x[t], 16)
            sp.dma_start(wgr[:], w_in[:, OFF_I:OFF_B].rearrange("(c p) n -> p c n", p=P)).then_inc(gates_w_in, 16)
            load_stage(0, 0, 0)
            for dst, off in ((bq, 0), (bk, DM), (bc_, OFF_C), (bx, OFF_X), (bb, OFF_B)):
                sp.dma_start(dst[:], column(b_in[off:off + DM]), allow_slow_non_contiguous=True).then_inc(consts_in, 16)
            sp.dma_start(mhg[:], column(mh_g), allow_slow_non_contiguous=True).then_inc(consts_in, 16)
            for k in range(TAPS):
                sp.dma_start(cw[:, k, :], column(conv_w[k]), allow_slow_non_contiguous=True).then_inc(consts_in, 16)
            sp.dma_start(bi[:], b_in[OFF_I:OFF_F].rearrange("(h a) -> h a", a=1)).then_inc(consts_in, 16)
            sp.dma_start(bf[:], b_in[OFF_F:OFF_B].rearrange("(h a) -> h a", a=1)).then_inc(consts_in, 16)
            for dst, v in ((bv, b_in[2 * DM:3 * DM]), (bo, b_in[3 * DM:4 * DM]), (lng, ln_g), (lnb, ln_b)):
                sp.dma_start(dst[:], v.partition_broadcast(P)).then_inc(consts_in, 16)
            with sp.Fori(0, NG) as g:
                for stage in range(1, ST):
                    load_stage(g, stage, 0)
                load_stage(g, 0, 1)

        POOL_TURN = 2 * NT

        @block.gpsimd
        def _(pool):
            own = Order(pool, pool_own, POOL_TURN)
            pool.memset(ident[:], 0.0).then_inc(consts_made, 1)
            pool.memset(mask[:], 0.0).then_inc(consts_made, 1)
            pool.memset(sel[:], 0.0).then_inc(consts_made, 1)
            pool.memset(identb[:], 0.0).then_inc(consts_made, 1)
            pool.wait_ge(consts_made, 4)
            for t in (ident, identb):
                pool.affine_select(out=t[:], in_=t[:], compare_op=ALU.not_equal, fill=1.0, base=0,
                                   pattern=[[-1, P]], channel_multiplier=1).then_inc(consts_made, 1)
            pool.affine_select(out=mask[:], in_=mask[:], compare_op=ALU.is_ge, fill=MASKED, base=0,
                               pattern=[[1, P]], channel_multiplier=-1).then_inc(consts_made, 1)
            pool.affine_select(out=sel[:], in_=sel[:], compare_op=ALU.not_equal, fill=1.0, base=0,
                               pattern=[[-1, NH], [0, P]], channel_multiplier=1).then_inc(consts_made, 1)
            pool.wait_ge(consts_in, N_CONSTS)

            def loads(g):
                def load_next(t):
                    row = (g + 1) % NG * GT + t * P
                    pool.dma_start(XN[:, t % 2], x[bass.ds(row, P)]).then_inc(x_in[t % 2], 16)

                wait_apart(pool, pool_idle, xt_ps, g * NT + NT)
                for t in range(2):
                    load_next(t)
                wait_apart(pool, pool_idle, conv_done, (g + 1) * NT)
                for t in range(NT):
                    pool.dma_start(R[:, t], x[bass.ds(g * GT + t * P, P)]).then_inc(res_in[t], 16)
                for t in range(2, NT):
                    wait_apart(pool, pool_idle, xt_ps, g * NT + NT + t - 1)
                    load_next(t)

            with pool.Fori(0, NG - 1) as g:
                loads(g)
                for t in range(NT):
                    pool.wait_ge(ln_done, g * NT + t + 1)
                    own.step(pool.tensor_tensor(R[:, t], R[:, t], lnb[:], ALU.add))
                    wait_apart(pool, pool_idle, *own.due(g))
                    row = g * GT + t * P
                    pool.dma_start(x1_dram[bass.ds(row, P)], R[:, t]).then_inc(x1_out, 16)
                wait_apart(pool, pool_idle, x1_out, (g + 1) * NT * 16)
                for t in range(NT):
                    own.step(pool.tensor_scalar(R[:, t], R[:, t], alpha, None, ALU.mult))
                    wait_apart(pool, pool_idle, *own.due(g))
                    pool.dma_start(acc_dram[bass.ds(g * GT + t * P, P)], R[:, t]).then_inc(xa_out, 16)
            assert own.n == POOL_TURN
            loads(NG - 1)
            for stored in (x1_out, xa_out):
                pool.wait_ge(stored, (NG - 1) * NT * 16)
            for k in range(2):
                pool.wait_ge(x_in[k], NG * NT // 2 * 16)

        ACT_TURN = 1 + NT + 2 + 2 * NT

        @block.scalar
        def _(act):
            own = Order(act, act_own, ACT_TURN)

            def split_stage(g, stage, after):
                n = g * ST + stage + after * ST
                use = g * NB + stage // 2 + after * NB
                act.wait_ge(raw_in[stage % 2], (use + 1) * 16)
                if stage % 2:
                    act.wait_ge(acc_full, g * FULL + stage // 2 * NT + after * FULL)
                else:
                    act.wait_ge(stage_used, use)
                act.activation(wh[:, stage % 2], raw[:, stage % 2], ACT.Copy).then_inc(split_h, 1)

            def take(g, stage, tiles):
                b = stage // 2
                if b not in BY_ACT or stage % 2 == 0:
                    if b == BB and stage % 2:
                        for t in tiles:
                            act.wait_ge(dve_out, g * N_DVE + dve_count(BB) * NT + t + 1)
                            act.activation(yTh[:, NH + t], YC[t % 2], ACT.Copy).then_inc(ych_done, 1)
                    return
                for t in tiles:
                    act.wait_ge(acc_full, g * FULL + b * NT + t + 1)
                    if b == QB:
                        act.activation(qT[:, t], acc[t][:], ACT.Identity, bias=bq[:, t:t + 1]).then_inc(act_out, 1)
                    else:
                        if t == 0:
                            act.wait_ge(xa_out, g * NT * 16)
                        act.activation(CT[:, t], acc[t][:], ACT.Identity, bias=bc_[:, t:t + 1]).then_inc(act_out, 1)

            def xt_tile(g, t, after):
                act.wait_ge(xt_ps, g * NT + t + 1 + after * NT)
                for k in range(2):
                    ins = act.activation(xTh[:, 4 * k:4 * k + 4, t * P:(t + 1) * P],
                                         aux[2 * (t % 2) + k][:].rearrange("p (c n) -> p c n", c=4), ACT.Copy)
                ins.then_inc(xt_h, 1)

            def sigmoid_o(g, t):
                act.wait_ge(dve_out, g * N_DVE + dve_count(OB) * NT + t + 1)
                own.step(act.activation(OG[:, t], OG[:, t], ACT.Exp, scale=-1.0))
                own.wait(g)
                own.step(act.activation(OG[:, t], OG[:, t], ACT.Ln, bias=1.0))
                own.wait(g)
                act.activation(OG[:, t], OG[:, t], ACT.Exp, scale=-1.0).then_inc(o_gate, 1)

            def extra(g, what, c):
                if what == "S1":
                    act.wait_ge(s1_ps, g * NT + c + 1)
                    for h in range(NH):
                        ins = act.activation(DT[:, h], aux[0][:, h * P:(h + 1) * P], ACT.Exp,
                                             bias=NAT[:, c, 3, h:h + 1])
                    ins.then_inc(dt_done, 1)
                if what == "Y" or (what == "S1" and c > 0):
                    cy = c if what == "Y" else c - 1
                    act.wait_ge(y_ps, g * NT + cy + 1)
                    a = aux[0] if what == "Y" else aux[3]
                    for h in range(NH):
                        ins = act.activation(yTh[:, h, cy * P:(cy + 1) * P], a[:, h * P:(h + 1) * P],
                                             ACT.Copy, scale=mhg[:, h:h + 1])
                    ins.then_inc(yh_done, 1)
                if what == "S2":
                    act.wait_ge(num_ps, g * NT + c + 1)
                    act.wait_ge(y_ps, g * NT + c)
                    for h in range(NH):
                        o = (h % 2) * W
                        ins = act.activation(NU[:, h], aux[2 + h // 2][:, o:o + W], ACT.Copy,
                                             scale=NAT[:, c, 0, h:h + 1])
                    ins.then_inc(inter_done, 1)
                    act.wait_ge(var_done, g * NT + c + 1)
                    own.step(act.activation(rstd[:], mv[:, :, 1], ACT.Ln, bias=eps[:, 0:1]))
                    own.wait(g)
                    act.activation(rstd[:], rstd[:], ACT.Exp, scale=-0.5).then_inc(rs_done, 1)
                if what == "X":
                    xt_tile(g, c, 1)

            act.add_instruction(mybir.InstLoadActFuncSet(name=nc.get_next_instruction_name(), ins=[], outs=[],
                                                         act_func_set_id=EXP_AND_LN))
            act.wait_ge(consts_made, 8)
            for t in range(NT // 2):
                xt_tile(0, t, 0)
            act.wait_ge(gates_w_in, 16)
            act.wait_ge(gates_w_split, 2)
            act.activation(gates_h[:, :, 0:NH], wgr[:, :, 0:NH], ACT.Copy)
            act.activation(gates_h[:, :, 32:], wgr[:, :, NH:], ACT.Copy).then_inc(gates_w_split, 1)
            for t in range(NT // 2, NT):
                xt_tile(0, t, 0)
            split_stage(0, 0, 0)
            act.wait_ge(dve_consts, 1)
            act.wait_ge(consts_in, N_CONSTS)
            with act.Fori(0, NG) as g:
                for stage in range(ST):
                    if stage == LAST_Y:
                        extra(g, "Y", NT - 1)
                    split_stage(g, (stage + 1) % ST, (stage + 1) // ST)
                    if stage == 0:
                        act.wait_ge(f_neg, g + 1)
                        own.step(act.activation(CM[:], CM[:], ACT.Exp))
                        own.wait(g)
                        act.activation(CM[:], CM[:], ACT.Ln, bias=1.0).then_inc(f_log, 1)
                    if stage == 2:
                        act.wait_ge(exps_in, g + 1)
                        act.activation(ROWS[0:NH], ROWS[0:NH], ACT.Exp)
                        act.activation(ROWS[32:32 + NH], ROWS[32:32 + NH], ACT.Exp, scale=-1.0)
                        act.activation(ROWS[64:64 + NH], ROWS[64:64 + NH], ACT.Exp)
                        act.activation(SPR[:], SPR[:], ACT.Exp).then_inc(rows_done, 1)
                    if stage in SIGMOID_STAGE[1:]:
                        sigmoid_o(g, SIGMOID_STAGE.index(stage))
                    if (stage, 0) in SLOT and stage != LAST_Y:
                        extra(g, *SLOT[(stage, 0)])
                    if stage == SIGMOID_STAGE[0]:
                        sigmoid_o(g, 0)
                    early = 0 if stage == Y_CONV else NT - 1
                    take(g, stage, range(early))
                    for t in range(1, NT):
                        if (stage, t) in SLOT and stage != LAST_Y:
                            extra(g, *SLOT[(stage, t)])
                    take(g, stage, range(early, NT))
                act.wait_ge(lvar_done, g + 1)
                own.step(act.activation(lrs[:], lmv[:, :, 1], ACT.Ln, bias=eps[:, 0:1]))
                own.wait(g)
                own.step(act.activation(lrs[:], lrs[:], ACT.Exp, scale=-0.5))
                own.wait(g)
                for t in range(NT):
                    act.wait_ge(ln_gained, g * NT + t + 1)
                    act.activation(R[:, t], R[:, t], ACT.Copy, scale=lrs[:, t:t + 1]).then_inc(ln_done, 1)
            assert own.n == ACT_TURN, own.n

        DVE_TURN = 58

        @block.vector
        def _(dve):
            own = Order(dve, dve_own, DVE_TURN)

            def split_stage(g, stage, after):
                n = g * ST + stage + after * ST
                dve.wait_ge(split_h, n + 1)
                dve.tensor_tensor(wl[:, stage % 2], raw[:, stage % 2], wh[:, stage % 2].bitcast(F32),
                                  ALU.subtract).then_inc(split_l, 1)

            def take(g, stage, tiles):
                b = stage // 2
                if stage % 2 == 0 or b in BY_ACT:
                    return
                for t in tiles:
                    dve.wait_ge(acc_full, g * FULL + b * NT + t + 1)
                    a = acc[t][:]
                    ah = acc[t][:].rearrange("p (h n) -> p h n", h=NH)
                    if b == KB:
                        dve.tensor_scalar(kT[:, t], a, bk[:, t:t + 1], DH ** -0.5, ALU.add, ALU.mult)\
                           .then_inc(dve_out, 1)
                    elif b == VB:
                        dve.tensor_tensor(V[:, t, :, 0:DH], ah, bv[:].rearrange("p (h n) -> p h n", h=NH),
                                          ALU.add).then_inc(dve_out, 1)
                    elif b == OB:
                        dve.tensor_tensor(OG[:, t], a, bo[:], ALU.add).then_inc(dve_out, 1)
                    elif b == XB:
                        dve.scalar_tensor_tensor(out=U[:, t, 2:], in0=a, scalar=bx[:, t:t + 1], in1=CT[:, t],
                                                 op0=ALU.add, op1=ALU.mult).then_inc(dve_out, 1)
                    elif b == BB:
                        if t > 1:
                            dve.wait_ge(conv_done, g * NT + t - 1)
                        dve.scalar_tensor_tensor(out=YC[t % 2], in0=a, scalar=bb[:, t:t + 1], in1=CT[:, t],
                                                 op0=ALU.add, op1=ALU.mult).then_inc(dve_out, 1)
                        if t:
                            y_conv_low(g, t - 1)
                        if t == NT - 1:
                            y_conv_low(g, t)
                    else:
                        n0 = (b - OUT0) * BANK
                        if b == OUT0:
                            dve.wait_ge(res_in[t], (g + 1) * 16)
                        dve.scalar_tensor_tensor(out=R[:, t, n0:n0 + BANK], in0=R[:, t, n0:n0 + BANK], scalar=alpha,
                                                 in1=a, op0=ALU.mult, op1=ALU.add).then_inc(dve_out, 1)
                if stage >= 2 * OUT0 + 1:
                    k = b - OUT0
                    dve.wait_ge(dve_out, g * N_DVE + dve_count(b) * NT + tiles.stop)
                    for t in tiles:
                        ins = dve.bn_stats(lstat[:, t, k], R[:, t, k * BANK:(k + 1) * BANK])
                    own.step(ins)

            def taps(g, t):
                own.step(dve.tensor_copy(U[:, t, 0:2], halo[:, t]))
                dve.wait_ge(dve_out, g * N_DVE + dve_count(XB) * NT + t + 1)
                own.wait(g)
                own.step(dve.tensor_copy(halo[:, t], U[:, t, GT:]))
                own.step(dve.tensor_scalar(CT[:, t], U[:, t, 0:GT], cw[:, 0, t:t + 1], None, ALU.mult))
                for k in range(1, TAPS):
                    own.wait(g)
                    own.step(dve.scalar_tensor_tensor(out=CT[:, t], in0=U[:, t, k:k + GT],
                                                      scalar=cw[:, k, t:t + 1], in1=CT[:, t],
                                                      op0=ALU.mult, op1=ALU.add))

            def y_conv_low(g, t):
                dve.wait_ge(ych_done, g * NT + t + 1)
                dve.tensor_tensor(yTl[:, NH + t], YC[t % 2], yTh[:, NH + t].bitcast(F32), ALU.subtract)\
                   .then_inc(conv_done, 1)

            def xt_tile(g, t, after):
                dve.wait_ge(xt_h, g * NT + t + 1 + after * NT)
                for k in range(2):
                    sl = (slice(None), slice(4 * k, 4 * k + 4), slice(t * P, (t + 1) * P))
                    ins = dve.tensor_tensor(xTl[sl], aux[2 * (t % 2) + k][:].rearrange("p (c n) -> p c n", c=4),
                                            xTh[sl].bitcast(F32), ALU.subtract)
                ins.then_inc(xt_done, 1)

            def extra(g, what, c):
                if what == "S1":
                    dve.wait_ge(s1_ps, g * NT + c + 1)
                    dve.tensor_tensor(KE[:], aux[2][:].rearrange("p (h n) -> p h n", h=NH),
                                      NAT[:, c, 2].unsqueeze(2).to_broadcast([P, NH, DH]), ALU.mult)
                    dve.wait_ge(dt_done, g * NT + c + 1)
                    dve.tensor_tensor(DT[:], DT[:], aux[1][:].rearrange("p (h n) -> p h n", h=NH),
                                      ALU.mult).then_inc(pt_done, 1)
                if what == "Y" or (what == "S1" and c > 0):
                    cy = c if what == "Y" else c - 1
                    dve.wait_ge(yh_done, g * NT + cy + 1)
                    a = aux[0] if what == "Y" else aux[3]
                    for h in range(NH):
                        sl = (slice(None), h, slice(cy * P, (cy + 1) * P))
                        ins = dve.scalar_tensor_tensor(out=yTl[sl], in0=a[:, h * P:(h + 1) * P],
                                                       scalar=mhg[:, h:h + 1], in1=yTh[sl].bitcast(F32),
                                                       op0=ALU.mult, op1=ALU.subtract)
                    ins.then_inc(yl_done, 1)
                if what == "S2":
                    dve.wait_ge(inter_done, g * NT + c + 1)
                    for k in range(2):
                        ins = dve.tensor_tensor(NU[:, 2 * k:2 * k + 2], NU[:, 2 * k:2 * k + 2],
                                                aux[k][:, 0:2 * W].rearrange("p (h n) -> p h n", h=2), ALU.add)
                    ins.then_inc(num_done, 1)
                    dve.wait_ge(num_done, g * NT + c + 1)
                    own.step(dve.scalar_tensor_tensor(out=den[:], in0=NU[:, :, DH], scalar=-1.0, in1=NU[:, :, DH],
                                                      op0=ALU.mult, op1=ALU.max))
                    own.wait(g)
                    own.step(dve.tensor_tensor(den[:], den[:], NAT[:, c, 1], ALU.max))
                    own.wait(g)
                    own.step(dve.reciprocal(den[:], den[:]))
                    own.wait(g)
                    own.step(dve.tensor_tensor(NU[:, :, 0:DH], NU[:, :, 0:DH],
                                               den[:].unsqueeze(2).to_broadcast([P, NH, DH]), ALU.mult))
                    own.wait(g)
                    for h in range(NH):
                        ins = dve.bn_stats(stat[:, h], NU[:, h, 0:DH])
                    own.step(ins)
                    wait_apart(dve, dve_idle, *own.due(g))
                    for h in range(NH):
                        ins = dve.bn_aggr(mv[:, h], stat[:, h])
                    ins.then_inc(var_done, 1)
                    dve.wait_ge(rs_done, g * NT + c + 1)
                    for h in range(NH):
                        ins = dve.tensor_scalar(NU[:, h, 0:DH], NU[:, h, 0:DH], mv[:, h, 0:1], rstd[:, h:h + 1],
                                                ALU.subtract, ALU.mult)
                    own.step(ins)
                    own.wait(g)
                    dve.wait_ge(o_gate, g * NT + c + 1)
                    dve.tensor_tensor(NU[:, :, 0:DH], NU[:, :, 0:DH], OG[:, c].rearrange("p (h n) -> p h n", h=NH),
                                      ALU.mult).then_inc(y_done, 1)
                if what == "S3":
                    dve.wait_ge(cl_ps, g * NT + c + 1)
                    for h in range(NH):
                        o = (h % 2) * W
                        ins = dve.scalar_tensor_tensor(out=CS[:, h], in0=CS[:, h], scalar=SPB[:, h, c:c + 1],
                                                       in1=aux[2 + h // 2][:, o:o + W], op0=ALU.mult, op1=ALU.add)
                    ins.then_inc(state_done, 1)
                if what == "X":
                    xt_tile(g, c, 1)

            for t in (wgh, wgl):
                dve.memset(t[:].bitcast(F32), 0.0).then_inc(gates_w_split, 1)
            dve.memset(zrow[:], 0.0)
            dve.memset(eps[:], LN_EPS)
            dve.memset(halo[:], 0.0)
            dve.memset(CS[:], 0.0)
            dve.memset(ROWS[:], 0.0)
            dve.memset(MS[:], 0.0)
            dve.memset(V[:, :, :, DH:], 1.0).then_inc(dve_consts, 1)
            for t in range(NT // 2):
                xt_tile(0, t, 0)
            dve.wait_ge(gates_w_split, 3)
            dve.tensor_tensor(gates_l[:, :, 0:NH], wgr[:, :, 0:NH], gates_h[:, :, 0:NH].bitcast(F32), ALU.subtract)
            dve.tensor_tensor(gates_l[:, :, 32:], wgr[:, :, NH:], gates_h[:, :, 32:].bitcast(F32),
                              ALU.subtract).then_inc(gates_w_split, 1)
            for t in range(NT // 2, NT):
                xt_tile(0, t, 0)
            split_stage(0, 0, 0)
            dve.wait_ge(dve_consts, 1)
            dve.wait_ge(consts_in, N_CONSTS)
            with dve.Fori(0, NG) as g:
                for stage in range(ST):
                    if stage == LAST_Y:
                        extra(g, "Y", NT - 1)
                    split_stage(g, (stage + 1) % ST, (stage + 1) // ST)
                    if stage == 0:
                        dve.wait_ge(gates_ps, g + 1)
                        dve.tensor_scalar(IG[:], aux[0][0:NH], bi[:, 0:1], None, ALU.add)
                        own.step(dve.tensor_scalar(FF[:], aux[0][32:32 + NH], bf[:, 0:1], None, ALU.add))
                        own.wait(g)
                        dve.scalar_tensor_tensor(out=CM[:], in0=FF[:], scalar=-1.0, in1=FF[:], op0=ALU.mult,
                                                 op1=ALU.min).then_inc(f_neg, 1)
                    if stage == 1:
                        dve.wait_ge(f_log, g + 1)
                        own.step(dve.scalar_tensor_tensor(out=FF[:], in0=FF[:], scalar=0.0, in1=CM[:], op0=ALU.min,
                                                          op1=ALU.subtract))
                        own.wait(g)
                        for c in range(NT):
                            s = slice(c * P, (c + 1) * P)
                            ins = dve.tensor_tensor_scan(FF[:, s], FF[:, s], zrow[:], 0.0, ALU.add, ALU.add)
                        own.step(ins)
                        own.wait(g)
                        own.step(dve.tensor_tensor(BR[:], IG[:], FF[:], ALU.subtract))
                        own.wait(g)
                        for c in range(NT):
                            s = slice(c * P, (c + 1) * P)
                            ins = dve.tensor_tensor_scan(CM[:, s], BR[:, s], zrow[:], LOWEST, ALU.max, ALU.add)
                        own.step(ins)
                        own.step(dve.tensor_copy(ROWS[96:96 + NH], BR[:]))
                        own.wait(g)
                        last = FF[:].rearrange("h (c n) -> h c n", c=NT)[:, :, P - 1]
                        bmax = CM[:].rearrange("h (c n) -> h c n", c=NT)[:, :, P - 1]
                        dve.wait_ge(exps_in, g)
                        own.step(dve.tensor_tensor_scan(MS[:, 1:], bmax, last, MS[:, 0:1], ALU.max, ALU.add))
                        own.wait(g)
                        before = MS[:, 0:NT].unsqueeze(2).to_broadcast([NH, NT, P])
                        cm3 = CM[:].rearrange("h (c n) -> h c n", c=NT)
                        own.step(dve.tensor_tensor(cm3, cm3, before, ALU.max))
                        own.step(dve.tensor_tensor(GM[:], last, MS[:, 1:], ALU.subtract))
                        own.wait(g)
                        dve.tensor_tensor(ROWS[0:NH].rearrange("h (c n) -> h c n", c=NT), before, cm3, ALU.subtract)
                        dve.tensor_tensor(ROWS[32:32 + NH], FF[:], CM[:], ALU.add)
                        dve.tensor_tensor(ROWS[64:64 + NH].rearrange("h (c n) -> h c n", c=NT),
                                          BR[:].rearrange("h (c n) -> h c n", c=NT),
                                          GM[:].unsqueeze(2).to_broadcast([NH, NT, P]), ALU.add)
                        dve.tensor_scalar(IG[:], CM[:], -1.0, None, ALU.mult)
                        own.step(dve.tensor_tensor(SPR[:], GM[:], MS[:, 0:NT], ALU.add))
                        own.wait(g)
                        dve.tensor_copy(MS[:, 0:1], MS[:, NT:]).then_inc(exps_in, 1)
                    if stage == 4:
                        dve.wait_ge(nat_ps, g + 1)
                        dve.tensor_copy(NAT[:], aux[3][:].rearrange("p (c q n) -> p c q n", c=NT, q=4)[:, :, :, 0:NH])
                        dve.tensor_copy(SPB[:], aux[1][:, 0:NH * NT].rearrange("p (h c) -> p h c", h=NH))\
                           .then_inc(nat_done, 1)
                    early = range(NT - 1)
                    if stage == Y_CONV:
                        dve.wait_ge(num_ps, g * NT + NT)
                        take(g, stage, range(1))
                        early = range(1, 1)
                    if (stage, 0) in SLOT and stage != LAST_Y:
                        extra(g, *SLOT[(stage, 0)])
                    if stage == Y_CONV - 1:
                        for t in range(NT // 2):
                            taps(g, t)
                    take(g, stage, early)
                    for t in range(1, NT):
                        if (stage, t) in SLOT and stage != LAST_Y:
                            extra(g, *SLOT[(stage, t)])
                    if stage == Y_CONV - 1:
                        for t in range(NT // 2, NT):
                            taps(g, t)
                    take(g, stage, range(early.stop, NT))
                wait_apart(dve, dve_idle, *own.due(g))
                for t in range(NT):
                    ins = dve.bn_aggr(lmv[:, t], lstat[:, t])
                ins.then_inc(lvar_done, 1)
                dve.wait_ge(lvar_done, g + 1)
                for t in range(NT):
                    dve.scalar_tensor_tensor(out=R[:, t], in0=R[:, t], scalar=lmv[:, t, 0:1], in1=lng[:],
                                             op0=ALU.subtract, op1=ALU.mult).then_inc(ln_gained, 1)
            assert own.n == DVE_TURN, own.n

        @block.tensor
        def _(pe):
            def three(out, ah, al, bh, bl, first, last):
                pe.matmul(out, ah, bh, start=first, stop=False)
                pe.matmul(out, ah, bl, start=False, stop=False)
                return pe.matmul(out, al, bh, start=False, stop=last)

            def tile(g, stage, t):
                b, half, s = stage // 2, stage % 2, stage % 2
                if half == 0:
                    if b == 0:
                        pe.wait_ge(dve_out, g * N_DVE)
                    elif previous(b) in BY_ACT:
                        pe.wait_ge(act_out, g * N_ACT + act_count(previous(b)) * NT + t + 1)
                    else:
                        pe.wait_ge(dve_out, g * N_DVE + dve_count(previous(b)) * NT + t + 1)
                sh, sl = (yTh, yTl) if b >= OUT0 else (xTh, xTl)
                for k in range(KH):
                    kc = half * KH + k
                    first, last = kc == 0, kc == KC - 1
                    cols = slice(t * P, (t + 1) * P)
                    if b in BY_CHANNEL:
                        ins = three(acc[t][:], wh[:, s, k, cols], wl[:, s, k, cols], sh[:, kc], sl[:, kc], first, last)
                    else:
                        ins = three(acc[t][:], sh[:, kc, cols], sl[:, kc, cols], wh[:, s, k], wl[:, s, k], first, last)
                if half:
                    ins.then_inc(acc_full, 1)
                elif t == NT - 1:
                    ins.then_inc(stage_used, 1)

            def xt_tile(g, t, after):
                n = g * NT + t + after * NT
                if after:
                    rows = XN[:, t % 2]
                    pe.wait_ge(x_in[t % 2], (g * (NT // 2) + t // 2 + 1) * 16)
                    if t == 0:
                        pe.wait_ge(yl_done, g * NT + NT)
                    elif t == 1:
                        pe.wait_ge(state_done, g * NT + NT)
                else:
                    rows = R[:, t]
                    pe.wait_ge(first_x[t], 16)
                if t >= 2:
                    pe.wait_ge(xt_done, n - 1)
                for k in range(KC):
                    ins = pe.transpose(aux[2 * (t % 2) + k // 4][:, (k % 4) * P:(k % 4 + 1) * P],
                                       rows[:, k * P:(k + 1) * P], ident[:])
                ins.then_inc(xt_ps, 1)

            def extra(g, what, c):
                cols = slice(c * P, (c + 1) * P)
                if what == "S1":
                    if c == 0:
                        pe.wait_ge(nat_done, g + 1)
                    else:
                        pe.wait_ge(num_done, g * NT + c)
                        pe.wait_ge(state_done, g * NT + c)
                        pe.wait_ge(y_done, g * NT + c)
                        for h in range(NH):
                            ins = pe.transpose(aux[3][:, h * P:(h + 1) * P], NU[:, h, 0:DH], ident[:])
                        ins.then_inc(y_ps, 1)
                    for h in range(NH):
                        pe.matmul(aux[0][:, h * P:(h + 1) * P], identb[:], mask[:], start=True, stop=False)
                        pe.matmul(aux[0][:, h * P:(h + 1) * P], sel[:, h], IG[:, cols], start=False, stop=True)
                    for h in range(NH):
                        pe.matmul(aux[1][:, h * P:(h + 1) * P], kT[:, h, cols], qT[:, h, cols], start=True, stop=True)
                    for h in range(NH):
                        ins = pe.transpose(aux[2][:, h * P:(h + 1) * P], kT[:, h, cols], ident[:])
                    ins.then_inc(s1_ps, 1)
                if what == "S2":
                    pe.wait_ge(pt_done, g * NT + c + 1)
                    if c:
                        pe.wait_ge(yl_done, g * NT + c)
                    for h in range(NH):
                        o = (h % 2) * W
                        pe.matmul(aux[h // 2][:, o:o + W], DT[:, h], V[:, c, h], start=True, stop=True)
                    for h in range(NH):
                        o = (h % 2) * W
                        ins = pe.matmul(aux[2 + h // 2][:, o:o + W], qT[:, h, cols], CS[:, h], start=True, stop=True)
                    ins.then_inc(num_ps, 1)
                if what == "S3":
                    pe.wait_ge(num_done, g * NT + c + 1)
                    for h in range(NH):
                        o = (h % 2) * W
                        ins = pe.matmul(aux[2 + h // 2][:, o:o + W], KE[:, h], V[:, c, h], start=True, stop=True)
                    ins.then_inc(cl_ps, 1)
                if what == "Y":
                    pe.wait_ge(y_done, g * NT + c + 1)
                    for h in range(NH):
                        ins = pe.transpose(aux[0][:, h * P:(h + 1) * P], NU[:, h, 0:DH], ident[:])
                    ins.then_inc(y_ps, 1)
                if what == "X":
                    xt_tile(g, c, 1)

            pe.wait_ge(consts_made, 8)
            for t in range(NT):
                xt_tile(0, t, 0)
            pe.wait_ge(dve_consts, 1)
            pe.wait_ge(gates_w_split, 4)
            with pe.Fori(0, NG) as g:
                pe.wait_ge(xt_done, g * NT + NT)
                for k in range(KC):
                    cols = slice(k * GC, k * GC + P)
                    ins = three(aux[0][:], wgh[:, cols], wgl[:, cols], xTh[:, k], xTl[:, k], k == 0, k == KC - 1)
                ins.then_inc(gates_ps, 1)
                for stage in range(ST):
                    pe.wait_ge(split_l, g * ST + stage + 1)
                    if stage == 4:
                        pe.wait_ge(rows_done, g + 1)
                        for c in range(NT):
                            pe.transpose(aux[3][:, c * P:(c + 1) * P], ROWS[:, c * P:(c + 1) * P], ident[:])
                        for h in range(NH):
                            ins = pe.matmul(aux[1][:, h * NT:(h + 1) * NT], sel[:, h], SPR[:], start=True, stop=True)
                        ins.then_inc(nat_ps, 1)
                    if stage == LAST_Y + 1:
                        pe.wait_ge(conv_done, (g + 1) * NT)
                    if stage == LAST_Y:
                        pe.wait_ge(yl_done, g * NT + NT - 1)
                    for t in range(NT):
                        if stage == LAST_Y and t == NT - 1:
                            pe.wait_ge(yl_done, g * NT + NT)
                        tile(g, stage, t)
                        if (stage, t) in SLOT:
                            extra(g, *SLOT[(stage, t)])
def route(nc, keep, x1_dram, acc_dram, router_w, router_b, w_gate, w_up, w_down, n_groups, alpha):
    S, D = x1_dram.shape
    NE = router_w.shape[1]
    PG = NE // n_groups
    NT = S // P
    KC = D // P
    NBW = keep.gather.shape[1]
    TOP = 2
    PAIR = 2 * P
    NP = S // PAIR
    MB = KC * PAIR // BANK

    ctx = ExitStack()
    with ctx:
        sb, ps, sem = tensors(nc, ctx, "route")
        X = sb("x1_rows", [P, 4, D])
        AX = sb("alpha_x1", [P, 4, D])
        XTh, XTl = (sb(n, [P, 2, KC, PAIR], F32R) for n in ("x1T_high", "x1T_low"))
        RW = sb("router_w", [P, KC, NE])
        RWh, RWl = (sb(n, [P, KC, P], F32R) for n in ("router_w_high", "router_w_low"))
        RB = sb("router_b", [NE, 1])
        LT = sb("logitsT", [NE, S])
        LG = sb("logits", [P, NT * NE])
        rows = sb("per_token", [P, 10, NT])
        HI, LO = (sb(n, [P, NT * n_groups, 2]) for n in ("pair_high", "pair_low"))
        G4 = sb("per_group", [P, 6, NT * n_groups])
        E16 = sb("per_expert", [P, 9, NT * NE])
        cnt = sb("per_count", [P, 4, NE])
        thr = sb("over_threshold", [P, NE, NT])
        slot_i = sb("slot_int", [P, 3, TOP * NT], I32)
        slot_f = sb("slot_parts", [P, 2, TOP * NT])
        gate = sb("gates", [P, TOP, NT])
        LOH = sb("slot_one_hot", [P, TOP * NT, P])
        RH = sb("block_one_hot", [P, TOP * NT, 2, NBW])
        BE = sb("block_over", [1, NBW, NE])
        tabf = sb("block_rows", [1, 6, NBW])
        tok = sb("slot_token", [P, 4, NBW])
        tri = sb("before", [P, P])
        ones = sb("ones", [P, P])
        gw = sb("group_weight", [P, n_groups])
        ew = sb("expert_weight", [P, NE])
        reset = sb("reset", [P, NE, NT])
        i128 = sb("iota_slot", [P, P])
        iblk = sb("iota_block", [P, NBW])
        ithr = sb("iota_threshold", [P, NT])
        tokp1 = sb("token_plus_1", [P, NT])
        dump = sb("dump_row", [P, 1])
        ii = sb("iota_int", [P, P], I32)
        zero = sb("zero_rows", [P, D])
        pt = [ps(f"xT{k}", [P, BANK]) for k in range(MB)]
        plg = ps("logits_psum", [P, BANK])
        pcs = [ps(f"counts{k}", [P, BANK]) for k in range(2)]
        psl = ps("slots_psum", [P, BANK])

        x_in = [sem(f"x1_in{k}") for k in range(4)]
        w_in = sem("router_in")
        rw_zero, rw_high, rw_low = sem("router_w_padded"), sem("router_w_high_ready"), sem("router_w_low_ready")
        ax_done = sem("alpha_x1_ready")
        ax_out = sem("alpha_x1_stored")
        late_done, late_out = sem("late_tile_done"), sem("late_x1_stored")
        made = sem("iotas_made")
        t_ps = sem("x1T_in_psum")
        t_hi = sem("x1T_high_ready")
        t_lo = sem("x1T_low_ready")
        l_ps = sem("logitsT_in_psum")
        l_done = sem("logitsT_taken")
        lg_ps = sem("logits_in_psum")
        centred = sem("logits_centred")
        expd = sem("exp_ready")
        m_done = sem("choices_ready")
        c_ps = sem("counts_in_psum")
        oh_done = sem("one_hots_ready")
        s_ps = sem("slots_in_psum")
        zero_out = sem("dump_rows_zeroed")
        own_sem = sem("dve_own")
        pool_sem = sem("pool_own")

        block = ctx.enter_context(nc.Block())

        @block.sync
        def _(sp):
            for t in range(2):
                sp.dma_start(X[:, t], x1_dram[t * P:(t + 1) * P]).then_inc(x_in[t], 16)
            sp.dma_start(RW[:], router_w.rearrange("(c p) n -> p c n", p=P)).then_inc(w_in, 16)
            sp.dma_start(RB[:], router_b.rearrange("(e a) -> e a", a=1)).then_inc(w_in, 16)
            for t in range(2, 4):
                sp.dma_start(X[:, t], x1_dram[t * P:(t + 1) * P]).then_inc(x_in[t], 16)
            with sp.Fori(1, NT // 4 - 1) as q:
                for t in range(4):
                    sp.wait_ge(t_ps, q * (2 * MB) + (t // 2 - 1) * MB)
                    sp.dma_start(X[:, t], x1_dram[bass.ds(q * 4 * P + t * P, P)]).then_inc(x_in[t], 16)
            sp.wait_ge(late_out, 4 * 16)
            for t in range(4):
                sp.wait_ge(t_ps, (NT // 2 - 2 + t // 2 - 1) * MB)
                sp.dma_start(X[:, t], x1_dram[S - (4 - t) * P:S - (3 - t) * P]).then_inc(x_in[t], 16)
            for part in range(3):
                load_part(sp, keep, part, w_gate[0:1], w_up[0:1], w_down[0:1], keep.first_in)
            sp.wait_ge(made, 1)
            sp.dma_start(acc_dram[S:S + P], zero[:]).then_inc(zero_out, 16)
            sp.wait_ge(zero_out, 16)

        @block.gpsimd
        def _(pool):
            for t in (RWh, RWl):
                pool.memset(t[:].bitcast(F32), 0.0).then_inc(rw_zero, 1)
            late = keep.conv_or_residual[:, 0:4 * D].rearrange("p (t n) -> p t n", t=4)
            for t in range(4):
                pool.tensor_tensor(late[:, t], late[:, t], keep.ln_bias[:], ALU.add).then_inc(late_done, 1)
                pool.wait_ge(late_done, t + 1)
                row = S - (4 - t) * P
                pool.dma_start(x1_dram[row:row + P], late[:, t]).then_inc(late_out, 16)
            pool.memset(zero[:], 0.0).then_inc(made, 1)
            own = Order(pool, pool_sem, 0)

            def iota(dst, src, **how):
                if own.n:
                    own.wait()
                own.step(pool.iota(src, **how))
                own.wait()
                own.step(pool.tensor_copy(dst, src))

            iota(i128[:], ii[:], pattern=[[1, P]], base=0, channel_multiplier=0)
            iota(iblk[:], ii[:, 0:NBW], pattern=[[1, NBW]], base=0, channel_multiplier=0)
            iota(ithr[:], ii[:, 0:NT], pattern=[[P, NT]], base=0, channel_multiplier=0)
            iota(tokp1[:], ii[:, 0:NT], pattern=[[P, NT]], base=1, channel_multiplier=1)
            iota(dump[:], ii[:, 0:1], pattern=[[1, 1]], base=S + 1, channel_multiplier=1)
            iota(gw[:], ii[:, 0:n_groups], pattern=[[-1, n_groups]], base=n_groups, channel_multiplier=0)
            iota(ew[:], ii[:, 0:NE], pattern=[[-1, NE]], base=NE, channel_multiplier=0)
            own.step(pool.memset(ones[:], 1.0))
            own.step(pool.memset(reset[:], 1.0))
            own.wait()
            own.step(pool.memset(reset[:, :, 0:1], 0.0))
            own.step(pool.affine_select(out=tri[:], in_=ones[:], compare_op=ALU.is_gt, fill=0.0, base=0,
                                        pattern=[[1, P]], channel_multiplier=-1))
            own.wait()
            pool.sem_inc(made, 1)

        @block.scalar
        def _(act):
            act.wait_ge(w_in, 32)
            act.wait_ge(rw_zero, 2)
            act.activation(RWh[:, :, 0:NE], RW[:], ACT.Copy).then_inc(rw_high, 1)
            with act.Fori(0, NP // 2) as q:
                for k in range(2):
                    p = 2 * q + k
                    for m in range(MB):
                        act.wait_ge(t_ps, p * MB + m + 1)
                        act.activation(XTh[:, k, 2 * m:2 * m + 2], pt[m][:].rearrange("p (c n) -> p c n", c=2),
                                       ACT.Copy).then_inc(t_hi, 1)
            act.wait_ge(centred, 1)
            act.activation(LG[:], LG[:], ACT.Exp).then_inc(expd, 1)
            for t in range(4):
                act.wait_ge(x_in[t], NT // 4 * 16)
                act.activation(AX[:, t], X[:, t], ACT.Copy, scale=alpha).then_inc(ax_done, 1)
                act.wait_ge(ax_done, t + 1)
                row = S - (4 - t) * P
                act.dma_start(acc_dram[row:row + P], AX[:, t]).then_inc(ax_out, 16)
            act.wait_ge(ax_out, 4 * 16)

        @block.tensor
        def _(pe):
            def transposes(p, k, use, first):
                for t in range(2):
                    pe.wait_ge(x_in[2 * k + t], (use + 1) * 16)
                for m in range(MB):
                    if not first:
                        pe.wait_ge(t_lo, (p - 1) * MB + m + 1)
                    for c in (2 * m, 2 * m + 1):
                        for t in range(2):
                            o = (c % 2) * PAIR + t * P
                            ins = pe.transpose(pt[m][:, o:o + P], X[:, 2 * k + t, c * P:(c + 1) * P], keep.ident[:])
                    ins.then_inc(t_ps, 1)

            def logits(p, k, first):
                if not first:
                    pe.wait_ge(l_done, p)
                out = plg[:, 0:PAIR]
                for c in range(KC):
                    if c % 2 == 0:
                        pe.wait_ge(t_lo, p * MB + c // 2 + 1)
                    pe.matmul(out, RWh[:, c], XTh[:, k, c], start=(c == 0), stop=False)
                    pe.matmul(out, RWh[:, c], XTl[:, k, c], start=False, stop=False)
                    ins = pe.matmul(out, RWl[:, c], XTh[:, k, c], start=False, stop=(c == KC - 1))
                ins.then_inc(l_ps, 1)

            transposes(0, 0, 0, True)
            pe.wait_ge(rw_low, 1)
            transposes(1, 1, 0, False)
            logits(0, 0, True)
            with pe.Fori(0, NP // 2 - 1) as q:
                transposes(2 * q + 2, 0, q + 1, False)
                logits(2 * q + 1, 1, False)
                transposes(2 * q + 3, 1, q + 1, False)
                logits(2 * q + 2, 0, False)
            logits(NP - 1, 1, False)
            pe.wait_ge(l_done, NP)
            for t in range(NT):
                ins = pe.transpose(pt[0][:, t * NE:(t + 1) * NE], LT[:, t * P:(t + 1) * P], keep.ident[0:NE, 0:NE])
            ins.then_inc(lg_ps, 1)
            pe.wait_ge(m_done, 1)
            pe.wait_ge(made, 2)
            pe.matmul(pcs[0][:, 0:NT * NE], tri[:], E16[:, 6], start=True, stop=True)
            pe.matmul(pcs[1][:, 0:NT * NE], ones[:], E16[:, 6], start=True, stop=True).then_inc(c_ps, 1)
            for n in range(TOP * NT):
                if n % NT == 0:
                    pe.wait_ge(oh_done, n // NT + 1)
                ins = pe.matmul(psl[:, 0:2 * NBW], LOH[:, n], RH[:, n].rearrange("p a b -> p (a b)"),
                                start=(n == 0), stop=(n == TOP * NT - 1))
            ins.then_inc(s_ps, 1)

        @block.vector
        def _(dve):
            own = Order(dve, own_sem, 0)

            def do(instruction):
                own.step(instruction)
                own.wait()

            dve.wait_ge(w_in, 32)
            dve.wait_ge(rw_high, 1)
            dve.tensor_tensor(RWl[:, :, 0:NE], RW[:], RWh[:, :, 0:NE].bitcast(F32), ALU.subtract).then_inc(rw_low, 1)

            def low(p, k):
                for m in range(MB):
                    dve.wait_ge(t_hi, p * MB + m + 1)
                    sl = (slice(None), k, slice(2 * m, 2 * m + 2))
                    dve.tensor_tensor(XTl[sl], pt[m][:].rearrange("p (c n) -> p c n", c=2), XTh[sl].bitcast(F32),
                                      ALU.subtract).then_inc(t_lo, 1)

            def take(p):
                dve.wait_ge(l_ps, p + 1)
                cols = bass.ds(p * PAIR, PAIR)
                dve.tensor_scalar(LT[:, cols], plg[0:NE, 0:PAIR], RB[:, 0:1], None, ALU.add)\
                   .then_inc(l_done, 1)

            low(0, 0)
            low(1, 1)
            take(0)
            with dve.Fori(0, NP // 2 - 1) as q:
                low(2 * q + 2, 0)
                take(2 * q + 1)
                low(2 * q + 3, 1)
                take(2 * q + 2)
            take(NP - 1)
            dve.wait_ge(lg_ps, 1)
            dve.wait_ge(made, 2)

            def by_token(a):
                return a.rearrange("p (t e) -> p t e", t=NT)

            def spread(a, *shape):
                return a.unsqueeze(2).to_broadcast([P, *shape])

            mx, sm, gm, km, t1, t2, rs = (rows[:, k] for k in range(7))
            lg = by_token(LG[:])
            raw_lg = by_token(pt[0][:, 0:NT * NE])
            do(dve.tensor_reduce(mx, raw_lg, AX_.X, ALU.max))
            dve.tensor_tensor(lg, raw_lg, spread(mx, NT, NE), ALU.subtract).then_inc(centred, 1)
            dve.wait_ge(expd, 1)
            do(dve.tensor_reduce(sm, lg, AX_.X, ALU.add))
            do(dve.reciprocal(sm, sm))
            do(dve.tensor_tensor(lg, lg, spread(sm, NT, NE), ALU.mult))
            four = LG[:].rearrange("p (g e) -> p g e", e=PG)
            own.step(dve.tensor_tensor(HI[:], four[:, :, 0:PG:2], four[:, :, 1:PG:2], ALU.max))
            do(dve.tensor_tensor(LO[:], four[:, :, 0:PG:2], four[:, :, 1:PG:2], ALU.min))
            own.step(dve.tensor_tensor(G4[:, 0], HI[:, :, 0], HI[:, :, 1], ALU.max))
            own.step(dve.tensor_tensor(G4[:, 1], HI[:, :, 0], HI[:, :, 1], ALU.min))
            do(dve.tensor_tensor(G4[:, 2], LO[:, :, 0], LO[:, :, 1], ALU.max))
            do(dve.tensor_tensor(G4[:, 1], G4[:, 1], G4[:, 2], ALU.max))
            do(dve.tensor_tensor(G4[:, 3], G4[:, 0], G4[:, 1], ALU.add))
            gsum, gsel = (G4[:, k].rearrange("p (t g) -> p t g", t=NT) for k in (3, 4))
            do(dve.tensor_reduce(gm, gsum, AX_.X, ALU.max))
            do(dve.tensor_tensor(gsel, gsum, spread(gm, NT, n_groups), ALU.is_equal))
            do(dve.tensor_tensor(gsel, gsel, gw[:].unsqueeze(1).to_broadcast([P, NT, n_groups]), ALU.mult))
            do(dve.tensor_reduce(km, gsel, AX_.X, ALU.max))
            do(dve.tensor_tensor(gsel, gsel, spread(km, NT, n_groups), ALU.is_equal))
            pm, oh1, oh2, key, slot, prod, both, exc, tot = (E16[:, k] for k in range(9))
            of_group = G4[:, 4].unsqueeze(2).to_broadcast([P, NT * n_groups, PG])
            own.step(dve.tensor_tensor(pm.rearrange("p (g e) -> p g e", e=PG), four, of_group, ALU.mult))
            do(dve.tensor_scalar(G4[:, 5], G4[:, 4], -1.0, None, ALU.add))
            do(dve.tensor_tensor(pm.rearrange("p (g e) -> p g e", e=PG), pm.rearrange("p (g e) -> p g e", e=PG),
                                 G4[:, 5].unsqueeze(2).to_broadcast([P, NT * n_groups, PG]), ALU.add))
            for top, oh in ((t1, oh1), (t2, oh2)):
                do(dve.tensor_reduce(top, by_token(pm), AX_.X, ALU.max))
                do(dve.tensor_tensor(by_token(key), by_token(pm), spread(top, NT, NE), ALU.is_equal))
                do(dve.tensor_tensor(by_token(key), by_token(key), ew[:].unsqueeze(1).to_broadcast([P, NT, NE]),
                                     ALU.mult))
                do(dve.tensor_reduce(km, by_token(key), AX_.X, ALU.max))
                do(dve.tensor_tensor(by_token(oh), by_token(key), spread(km, NT, NE), ALU.is_equal))
                if oh is oh1:
                    do(dve.scalar_tensor_tensor(out=pm, in0=oh1, scalar=-4.0, in1=pm, op0=ALU.mult, op1=ALU.add))
            dve.tensor_tensor(both, oh1, oh2, ALU.add).then_inc(m_done, 1)
            do(dve.tensor_tensor(rs, t1, t2, ALU.add))
            do(dve.reciprocal(rs, rs))
            own.step(dve.tensor_tensor(gate[:, 0], t1, rs, ALU.mult))
            own.step(dve.tensor_tensor(gate[:, 1], t2, rs, ALU.mult))
            dve.wait_ge(c_ps, 1)
            et = "p (e t) -> p e t"
            do(dve.tensor_copy(tot.rearrange(et, e=NE), pcs[1][:, 0:NT * NE].rearrange("p (t e) -> p e t", t=NT)))
            do(dve.tensor_tensor_scan(exc, reset[:].rearrange("p e t -> p (e t)"), tot, 0.0, ALU.mult, ALU.add))
            count, blocks, end, start = (cnt[:, k] for k in range(4))
            do(dve.tensor_copy(count, exc.rearrange(et, e=NE)[:, :, NT - 1]))
            own.step(dve.tensor_tensor(thr[:], spread(count, NE, NT), ithr[:].unsqueeze(1).to_broadcast([P, NE, NT]),
                                       ALU.is_gt))
            do(dve.tensor_tensor(exc, exc, tot, ALU.subtract))
            do(dve.tensor_reduce(blocks, thr[:], AX_.X, ALU.add))
            do(dve.tensor_tensor_scan(end, ones[:, 0:NE], blocks, 0.0, ALU.mult, ALU.add))
            do(dve.tensor_tensor(start, end, blocks, ALU.subtract))
            do(dve.tensor_scalar(start, start, float(P), None, ALU.mult))
            do(dve.tensor_tensor(exc.rearrange(et, e=NE), exc.rearrange(et, e=NE), spread(start, NE, NT), ALU.add))
            do(dve.tensor_tensor(by_token(slot), pcs[0][:, 0:NT * NE].rearrange("p (t e) -> p t e", t=NT),
                                 exc.rearrange("p (e t) -> p t e", e=NE), ALU.add))
            for k, oh in enumerate((oh1, oh2)):
                do(dve.tensor_tensor(prod, oh, slot, ALU.mult))
                do(dve.tensor_reduce(rows[:, 8 + k], by_token(prod), AX_.X, ALU.add))
            do(dve.tensor_copy(slot_i[:, 0], rows[:, 8:10].rearrange("p a b -> p (a b)")))
            own.step(dve.tensor_scalar(slot_i[:, 1], slot_i[:, 0], 7, None, ALU.arith_shift_right))
            do(dve.tensor_scalar(slot_i[:, 2], slot_i[:, 0], P - 1, None, ALU.bitwise_and))
            do(dve.tensor_copy(slot_f[:], slot_i[:, 1:3]))
            for k in range(TOP):
                half = slice(k * NT, (k + 1) * NT)
                place, of_block = (slot_f[:, a, half].unsqueeze(2) for a in (1, 0))
                own.step(dve.tensor_tensor(RH[:, half, 1], iblk[:].unsqueeze(1).to_broadcast([P, NT, NBW]),
                                           of_block.to_broadcast([P, NT, NBW]), ALU.is_equal))
                do(dve.tensor_tensor(LOH[:, half], i128[:].unsqueeze(1).to_broadcast([P, NT, P]),
                                     place.to_broadcast([P, NT, P]), ALU.is_equal))
                do(dve.tensor_tensor(RH[:, half, 0], RH[:, half, 1], tokp1[:].unsqueeze(2).to_broadcast([P, NT, NBW]),
                                     ALU.mult))
                do(dve.tensor_tensor(RH[:, half, 1], RH[:, half, 1],
                                     gate[:, k].unsqueeze(2).to_broadcast([P, NT, NBW]), ALU.mult))
                dve.sem_inc(oh_done, 1)
            be, fresh, before, earlier, active, pairs = (tabf[:, k] for k in range(6))
            do(dve.tensor_tensor(BE[:], end[0:1].unsqueeze(1).to_broadcast([1, NBW, NE]),
                                 iblk[0:1].unsqueeze(2).to_broadcast([1, NBW, NE]), ALU.is_le))
            do(dve.tensor_reduce(be, BE[:], AX_.X, ALU.add))
            do(dve.tensor_scalar(be, be, float(NE - 1), None, ALU.min))
            own.step(dve.memset(fresh[:, 0:1], 1.0))
            own.step(dve.memset(pairs, 0.0))
            own.step(dve.tensor_scalar(active, iblk[0:1], end[0:1, NE - 1:NE], None, ALU.is_lt))
            do(dve.tensor_tensor(fresh[:, 1:], be[:, 1:], be[:, 0:NBW - 1], ALU.not_equal))
            own.step(dve.tensor_tensor(fresh[:, 1:], fresh[:, 1:], active[:, 1:], ALU.mult))
            do(dve.tensor_reduce(pairs[:, 0:1], active[:, 1::2], AX_.X, ALU.add))
            do(dve.tensor_tensor_scan(before, ones[0:1, 0:NBW], fresh, -1.0, ALU.mult, ALU.add))
            do(dve.tensor_scalar(earlier, before, -1.0, 0.0, ALU.add, ALU.max))
            own.step(dve.tensor_copy(keep.table[:], tabf[:]))
            dve.wait_ge(s_ps, 1)
            own.step(dve.tensor_copy(tok[:, 0], psl[:, 0:NBW]))
            do(dve.tensor_copy(keep.gate[:], psl[:, NBW:2 * NBW]))
            own.step(dve.tensor_scalar(tok[:, 1], tok[:, 0], -1.0, 0.0, ALU.add, ALU.max))
            own.step(dve.tensor_scalar(tok[:, 2], tok[:, 0], 0.0, None, ALU.is_equal))
            do(dve.tensor_scalar(tok[:, 3], tok[:, 0], -1.0, None, ALU.add))
            do(dve.scalar_tensor_tensor(out=tok[:, 3], in0=tok[:, 2], scalar=dump[:, 0:1], in1=tok[:, 3],
                                        op0=ALU.mult, op1=ALU.add))
            dve.tensor_copy(keep.gather[:], tok[:, 1])
            do(dve.tensor_copy(keep.scatter[:], tok[:, 3]))


def load_part(engine, keep, part, w_gate, w_up, w_down, sem):
    D, F = w_gate.shape[1], w_gate.shape[2]
    half = D // 2
    for k in range(2):
        if part < 2:
            src = (w_gate, w_up)[k][:, part * half:(part + 1) * half, :].rearrange("a (c p) n -> p (a c) n", p=P)
            dst = keep.raw[:, 2 * part:2 * part + 2].rearrange("p a c n -> p (a c) n")[:, :, k * F:(k + 1) * F]
        else:
            src = w_down[:, 2 * k * P:2 * (k + 1) * P, :].rearrange("a (c p) n -> p (a c) n", p=P)
            dst = keep.raw[:, D // (2 * P) + k]
        engine.dma_start(dst, src).then_inc(sem, 16)


def experts(nc, keep, x1_dram, acc_dram, w_gate, w_up, w_down):
    D = x1_dram.shape[1]
    NE, _, F = w_gate.shape
    KC = D // P
    FC = F // P
    NBLK = keep.gather.shape[1] - 2
    NGU, NDN = KC // 2, FC // 2
    NPAIR = NGU + NDN
    assert F == BANK and D == 2 * BANK and NBLK % 2 == 1

    ctx = ExitStack()
    with ctx:
        sb, ps, sem = tensors(nc, ctx, "moe")
        raw = keep.raw
        wh, wl = (sb(n, [P, NPAIR, 2, D], F32R) for n in ("w_high", "w_low"))
        X = sb("x_rows", [P, 2, D])
        xTh, xTl = (sb(n, [P, 2, KC, P], F32R) for n in ("xT_high", "xT_low"))
        sig = sb("sigmoid", [P, F])
        hid = sb("hidden", [P, F])
        hTh, hTl = (sb(n, [P, FC, P], F32R) for n in ("hiddenT_high", "hiddenT_low"))
        Y = sb("y_rows", [P, 2, D])
        gi, si = (sb(n, [P, 2], I32) for n in ("gather_index", "scatter_index"))
        pg, pu = ps("gate_psum", [P, BANK]), ps("up_psum", [P, BANK])
        py = [ps(f"y_psum{k}", [P, BANK]) for k in range(2)]
        px = [ps(f"xT_psum{k}", [P, BANK]) for k in range(2)]
        ph = ps("hiddenT_psum", [P, BANK])

        raw_in = [sem(f"w_raw_in{k}") for k in range(3)]
        gu_h, gu_l = sem("gate_up_high_ready"), sem("gate_up_low_ready")
        dn_h, dn_l = sem("down_high_ready"), sem("down_low_ready")
        gu_used, dn_used = sem("gate_up_used"), sem("down_used")
        x_in = [sem(f"x_rows_in{k}") for k in range(2)]
        x_ps, xh_done, xl_done = sem("xT_in_psum"), sem("xT_high_ready"), sem("xT_low_ready")
        sig_done, hid_done = sem("sigmoid_ready"), sem("hidden_ready")
        ht_ps, hh_done, hl_done = sem("hiddenT_in_psum"), sem("hiddenT_high_ready"), sem("hiddenT_low_ready")
        y_act, y_dve = sem("y_first_half"), sem("y_second_half")
        added, y_free = sem("y_added"), sem("y_slot_free")
        other_in, first_ready, last_index = sem("other_first_in"), sem("first_weights_in"), sem("last_index_ready")
        dve_own, pool_own, pool_idle = sem("dve_own"), sem("pool_own"), sem("pool_wait_carrier")

        def entry(engine, row, b):
            most = (NE - 1, 1, NE, NE, 1, NBLK // 2)[row]
            return engine.value_load(keep.table[0:1, row, bass.ds(b, 1)], min_val=0, max_val=most)

        def last_block(engine):
            return 2 * entry(engine, 5, 0)

        block = ctx.enter_context(nc.Block())

        @block.sync
        def _(sp):
            def views(e):
                return [w[bass.ds(e, 1)] for w in (w_gate, w_up, w_down)]

            sp.wait_ge(keep.first_in, 6 * 16)
            e = entry(sp, 0, 0)
            with sp.If(e):
                for part in range(3):
                    load_part(sp, keep, part, *views(e), other_in)
                sp.wait_ge(other_in, 6 * 16)
            sp.sem_inc(first_ready, 1)
            with sp.Fori(1, NBLK) as b:
                fresh = entry(sp, 1, b)
                with sp.If(fresh):
                    e, n, before = entry(sp, 0, b), entry(sp, 2, b), entry(sp, 3, b)
                    for part in range(3):
                        if part < 2:
                            sp.wait_ge(gu_l, before * NGU + (part + 1) * 2)
                        else:
                            sp.wait_ge(dn_l, n * NDN)
                        load_part(sp, keep, part, *views(e), raw_in[part])

        @block.gpsimd
        def _(pool):
            POOL_TURN = 4
            own = Order(pool, pool_own, POOL_TURN, 3)

            def gather(b, k):
                pool.indirect_dma_start(out=X[:, k], out_offset=None, in_=x1_dram,
                                        in_offset=bass.IndirectOffsetOnAxis(ap=gi[:, k:k + 1], axis=0))\
                    .then_inc(x_in[k], 16)

            def scatter(k):
                pool.indirect_dma_start(out=acc_dram, out_offset=bass.IndirectOffsetOnAxis(ap=si[:, k:k + 1], axis=0),
                                        in_=Y[:, k], in_offset=None, compute_op=ALU.add).then_inc(added, 16)

            for k in range(2):
                pool.tensor_copy(gi[:, k:k + 1], keep.gather[:, k:k + 1]).then_inc(pool_own, 1)
            pool.wait_ge(pool_own, 2)
            for k in range(2):
                gather(k, k)
            pool.wait_ge(x_ps, 1)
            pool.tensor_copy(gi[:, 0:1], keep.gather[:, 2:3]).then_inc(pool_own, 1)
            pool.wait_ge(pool_own, 3)
            gather(2, 0)
            with pool.Fori(0, NBLK // 2) as j:
                on = entry(pool, 4, 2 * j + 1)
                with pool.If(on):
                    for i in range(2):
                        b = 2 * j + 1 + i
                        k = (1 + i) % 2
                        pool.wait_ge(x_ps, b + 1)
                        own.step(pool.tensor_copy(gi[:, k:k + 1], keep.gather[:, bass.ds(b + 2, 1)]))
                        wait_apart(pool, pool_idle, *own.due(j))
                        gather(b + 2, k)
                        wait_apart(pool, y_free, added, (b - 1) * 16)
                        own.step(pool.tensor_copy(si[:, 1 - k:2 - k], keep.scatter[:, bass.ds(b - 1, 1)]))
                        pool.wait_ge(y_act, b)
                        pool.wait_ge(y_dve, b)
                        wait_apart(pool, pool_idle, *own.due(j))
                        scatter(1 - k)
            half = entry(pool, 5, 0)
            last = 2 * half
            wait_apart(pool, y_free, added, last * 16)
            pool.tensor_copy(si[:, 0:1], keep.scatter[:, bass.ds(last, 1)]).then_inc(last_index, 1)
            pool.wait_ge(last_index, 1)
            wait_apart(pool, pool_idle, y_act, last + 1)
            wait_apart(pool, pool_idle, y_dve, last + 1)
            scatter(0)
            wait_apart(pool, pool_idle, added, (last + 1) * 16)
            wait_apart(pool, pool_idle, x_in[0], (half + 2) * 16)
            wait_apart(pool, pool_idle, x_in[1], (half + 1) * 16)
            assert own.n == POOL_TURN

        @block.scalar
        def _(act):
            def x_high(b, k):
                act.wait_ge(x_ps, b + 1)
                for c in range(2):
                    ins = act.activation(xTh[:, k, 4 * c:4 * c + 4], px[c][:].rearrange("p (c n) -> p c n", c=4),
                                         ACT.Copy)
                ins.then_inc(xh_done, 1)

            def split(b, n, pairs, free):
                for u in pairs:
                    gu = u < NGU
                    if not free:
                        act.wait_ge(first_ready, 1)
                    else:
                        act.wait_ge(raw_in[u // 2], n * 32)
                    if free:
                        if gu:
                            act.wait_ge(gu_used, (b - 1) * NGU + u + 1)
                        else:
                            act.wait_ge(dn_used, (b - 1) * NDN + u - NGU + 1)
                    act.activation(wh[:, u], raw[:, u], ACT.Copy).then_inc(gu_h if gu else dn_h, 1)

            def hidden(b):
                act.wait_ge(gu_used, (b + 1) * NGU)
                if not isinstance(b, int):
                    act.wait_ge(hid_done, b)
                act.activation(sig[:], pg[:], ACT.Sigmoid).then_inc(sig_done, 1)

            def y_half(b, k):
                act.wait_ge(dn_used, (b + 1) * NDN)
                act.wait_ge(y_free, b)
                act.activation(Y[:, k, 0:BANK], py[0][:], ACT.Copy,
                               scale=keep.gate[:, bass.ds(b, 1)]).then_inc(y_act, 1)

            def hT_high(b):
                act.wait_ge(ht_ps, b + 1)
                act.activation(hTh[:], ph[:].rearrange("p (c n) -> p c n", c=FC), ACT.Copy).then_inc(hh_done, 1)

            split(0, 0, range(2), False)
            x_high(0, 0)
            split(0, 0, range(2, NGU), False)
            split(0, 0, range(NGU, NPAIR), False)
            first, n = entry(act, 1, 1), entry(act, 2, 1)
            with act.If(first):
                split(1, n, range(0, NGU), True)
            hidden(0)
            x_high(1, 1)
            hT_high(0)
            with act.Fori(0, NBLK // 2) as j:
                on = entry(act, 4, 2 * j + 1)
                with act.If(on):
                    for i in range(2):
                        b = 2 * j + 1 + i
                        k = (1 + i) % 2
                        x_high(b + 1, 1 - k)
                        first, n = entry(act, 1, b + 1), entry(act, 2, b + 1)
                        with act.If(first):
                            split(b + 1, n, range(0, 2), True)
                        hidden(b)
                        with act.If(first):
                            split(b + 1, n, range(2, NGU), True)
                        y_half(b - 1, 1 - k)
                        hT_high(b)
                        first, n = entry(act, 1, b), entry(act, 2, b)
                        with act.If(first):
                            split(b, n, range(NGU, NPAIR), True)
            y_half(last_block(act), 0)

        @block.vector
        def _(dve):
            DVE_TURN = 2
            own = Order(dve, dve_own, DVE_TURN, 1)

            def x_low(b, k):
                dve.wait_ge(xh_done, b + 1)
                for c in range(2):
                    sl = (slice(None), k, slice(4 * c, 4 * c + 4))
                    ins = dve.tensor_tensor(xTl[sl], px[c][:].rearrange("p (c n) -> p c n", c=4),
                                            xTh[sl].bitcast(F32), ALU.subtract)
                ins.then_inc(xl_done, 1)

            def split(n, pairs):
                for u in pairs:
                    gu = u < NGU
                    if gu:
                        dve.wait_ge(gu_h, n * NGU + u + 1)
                    else:
                        dve.wait_ge(dn_h, n * NDN + u - NGU + 1)
                    dve.tensor_tensor(wl[:, u], raw[:, u], wh[:, u].bitcast(F32), ALU.subtract)\
                       .then_inc(gu_l if gu else dn_l, 1)

            def hidden(b, turn):
                dve.wait_ge(sig_done, b + 1)
                if not isinstance(b, int):
                    dve.wait_ge(ht_ps, b)
                ins = dve.tensor_tensor(hid[:], pg[:], sig[:], ALU.mult)
                if turn is None:
                    ins.then_inc(dve_own, 1)
                    dve.wait_ge(dve_own, 1)
                else:
                    own.step(ins)
                    own.wait(turn)
                dve.tensor_tensor(hid[:], hid[:], pu[:], ALU.mult).then_inc(hid_done, 1)

            def y_half(b, k):
                dve.wait_ge(dn_used, (b + 1) * NDN)
                dve.wait_ge(y_free, b)
                dve.tensor_scalar(Y[:, k, BANK:], py[1][:], keep.gate[:, bass.ds(b, 1)], None,
                                  ALU.mult).then_inc(y_dve, 1)

            def hT_low(b):
                dve.wait_ge(hh_done, b + 1)
                dve.tensor_tensor(hTl[:], ph[:].rearrange("p (c n) -> p c n", c=FC), hTh[:].bitcast(F32),
                                  ALU.subtract).then_inc(hl_done, 1)

            split(0, range(2))
            x_low(0, 0)
            split(0, range(2, NGU))
            split(0, range(NGU, NPAIR))
            first, n = entry(dve, 1, 1), entry(dve, 2, 1)
            with dve.If(first):
                split(n, range(0, NGU))
            hidden(0, None)
            x_low(1, 1)
            hT_low(0)
            with dve.Fori(0, NBLK // 2) as j:
                on = entry(dve, 4, 2 * j + 1)
                with dve.If(on):
                    for i in range(2):
                        b = 2 * j + 1 + i
                        k = (1 + i) % 2
                        x_low(b + 1, 1 - k)
                        first, n = entry(dve, 1, b + 1), entry(dve, 2, b + 1)
                        with dve.If(first):
                            split(n, range(0, 2))
                        hidden(b, j)
                        with dve.If(first):
                            split(n, range(2, NGU))
                        y_half(b - 1, 1 - k)
                        hT_low(b)
                        first, n = entry(dve, 1, b), entry(dve, 2, b)
                        with dve.If(first):
                            split(n, range(NGU, NPAIR))
            y_half(last_block(dve), 0)
            assert own.n == DVE_TURN

        @block.tensor
        def _(pe):
            def three(out, ah, al, bh, bl, first, last):
                pe.matmul(out, ah, bh, start=first, stop=False)
                pe.matmul(out, ah, bl, start=False, stop=False)
                return pe.matmul(out, al, bh, start=False, stop=last)

            def turn_x(b, k, use):
                pe.wait_ge(x_in[k], (use + 1) * 16)
                if not isinstance(b, int) or b:
                    pe.wait_ge(xl_done, b)
                for c in range(KC):
                    ins = pe.transpose(px[c // 4][:, (c % 4) * P:(c % 4 + 1) * P], X[:, k, c * P:(c + 1) * P],
                                       keep.ident[:])
                ins.then_inc(x_ps, 1)

            def gate_up(b, k, n):
                pe.wait_ge(xl_done, b + 1)
                if not isinstance(b, int):
                    pe.wait_ge(hid_done, b)
                for u in range(NGU):
                    pe.wait_ge(gu_l, n * NGU + u + 1)
                    for c in range(2):
                        kc = 2 * u + c
                        for out, s in ((pg, slice(0, F)), (pu, slice(F, 2 * F))):
                            ins = three(out[:], xTh[:, k, kc], xTl[:, k, kc], wh[:, u, c, s], wl[:, u, c, s],
                                        kc == 0, kc == KC - 1)
                    ins.then_inc(gu_used, 1)

            def down(b, n):
                pe.wait_ge(hl_done, b + 1)
                if not isinstance(b, int) or b:
                    pe.wait_ge(y_act, b)
                    pe.wait_ge(y_dve, b)
                for u in range(NDN):
                    pe.wait_ge(dn_l, n * NDN + u + 1)
                    for c in range(2):
                        kc = 2 * u + c
                        for q in range(2):
                            s = slice(q * BANK, (q + 1) * BANK)
                            ins = three(py[q][:], hTh[:, kc], hTl[:, kc], wh[:, NGU + u, c, s], wl[:, NGU + u, c, s],
                                        kc == 0, kc == FC - 1)
                    ins.then_inc(dn_used, 1)

            def turn_hidden(b):
                pe.wait_ge(hid_done, b + 1)
                if not isinstance(b, int):
                    pe.wait_ge(hl_done, b)
                for c in range(FC):
                    ins = pe.transpose(ph[:, c * P:(c + 1) * P], hid[:, c * P:(c + 1) * P], keep.ident[:])
                ins.then_inc(ht_ps, 1)

            turn_x(0, 0, 0)
            gate_up(0, 0, 0)
            turn_x(1, 1, 0)
            turn_hidden(0)
            with pe.Fori(0, NBLK // 2) as j:
                on = entry(pe, 4, 2 * j + 1)
                with pe.If(on):
                    for i in range(2):
                        b = 2 * j + 1 + i
                        k = (1 + i) % 2
                        turn_x(b + 1, 1 - k, j + 1)
                        gate_up(b, k, entry(pe, 2, b))
                        down(b - 1, entry(pe, 2, b - 1))
                        turn_hidden(b)
            last = last_block(pe)
            down(last, entry(pe, 2, last))


def final_norm(nc, acc_dram, ln_g, ln_b, out):
    S, D = out.shape
    TT = 2
    SL = 4
    TURNS = S // (TT * P)
    assert TURNS % SL == 0

    ctx = ExitStack()
    with ctx:
        sb, ps, sem = tensors(nc, ctx, "norm")
        R = sb("rows", [P, SL, TT, D])
        O = sb("normed", [P, SL, TT, D])
        lng, lnb = (sb(n, [P, D]) for n in ("ln_gain", "ln_bias"))
        stats = sb("stats", [P, SL, TT, 2, 6])
        mv = sb("mean_var", [P, SL, TT, 2])
        rstd, shift = (sb(n, [P, SL, TT]) for n in ("rstd", "shift"))
        eps = sb("eps", [P, 1])
        r_in = [[sem(f"rows_in{s}{k}") for k in range(TT)] for s in range(SL)]
        ln_in = sem("ln_in")
        eps_made, var_done = sem("eps_made"), sem("var_ready")
        n_done, g_done, o_done = sem("normalised"), sem("gain_applied"), sem("bias_added")
        stored = [sem(f"out_stored{s}") for s in range(SL)]
        dve_own, act_own = sem("dve_own"), sem("act_own")
        dve_idle = sem("dve_wait_carrier")
        block = ctx.enter_context(nc.Block())

        @block.sync
        def _(sp):
            def load(turn):
                for k in range(TT):
                    if turn >= SL:
                        sp.wait_ge(n_done, (turn - SL) * TT + k + 1)
                    row = (turn * TT + k) * P
                    sp.dma_start(R[:, turn % SL, k], acc_dram[row:row + P]).then_inc(r_in[turn % SL][k], 16)

            def store(turn):
                for k in range(TT):
                    sp.wait_ge(o_done, turn * TT + k + 1)
                    row = (turn * TT + k) * P
                    sp.dma_start(out[row:row + P], O[:, turn % SL, k]).then_inc(stored[turn % SL], 16)

            load(0)
            for v, dst in ((ln_g, lng), (ln_b, lnb)):
                sp.dma_start(dst[:], v.partition_broadcast(P)).then_inc(ln_in, 16)
            for turn in range(1, SL):
                load(turn)
            for turn in range(TURNS):
                if turn + SL < TURNS:
                    load(turn + SL)
                store(turn)
            for s in range(SL):
                sp.wait_ge(stored[s], TURNS // SL * TT * 16)

        @block.scalar
        def _(act):
            own = Order(act, act_own, 4 * SL)
            act.add_instruction(mybir.InstLoadActFuncSet(name=nc.get_next_instruction_name(), ins=[], outs=[],
                                                         act_func_set_id=EXP_AND_LN))
            act.wait_ge(eps_made, 1)
            with act.Fori(0, TURNS // SL) as j:
                for s in range(SL):
                    act.wait_ge(var_done, SL * j + s + 1)
                    own.step(act.activation(rstd[:, s], mv[:, s, :, 1], ACT.Ln, bias=eps[:, 0:1]))
                    own.wait(j)
                    own.step(act.activation(rstd[:, s], rstd[:, s], ACT.Exp, scale=-0.5))
                    own.step(act.activation(shift[:, s], mv[:, s, :, 0], ACT.Copy, scale=-1.0))
                    own.wait(j)
                    for k in range(TT):
                        ins = act.activation(shift[:, s, k:k + 1], shift[:, s, k:k + 1], ACT.Copy,
                                             scale=rstd[:, s, k:k + 1])
                    own.step(ins)
                    own.wait(j)
                    act.wait_ge(stored[s], j * (TT * 16))
                    for k in range(TT):
                        act.activation(O[:, s, k], R[:, s, k], ACT.Identity, bias=shift[:, s, k:k + 1],
                                       scale=rstd[:, s, k:k + 1]).then_inc(n_done, 1)
            assert own.n == own.per_turn

        @block.vector
        def _(dve):
            def variances(turn, s, use):
                for k in range(TT):
                    dve.wait_ge(r_in[s][k], (use + 1) * 16)
                    for h in range(2):
                        ins = dve.bn_stats(stats[:, s, k, h], R[:, s, k, h * BANK:(h + 1) * BANK])
                ins.then_inc(dve_own, 1)
                wait_apart(dve, dve_idle, dve_own, turn + 1)
                for k in range(TT):
                    ins = dve.bn_aggr(mv[:, s, k], stats[:, s, k])
                ins.then_inc(var_done, 1)

            dve.memset(eps[:], LN_EPS).then_inc(eps_made, 1)
            variances(0, 0, 0)
            dve.wait_ge(ln_in, 32)
            with dve.Fori(0, TURNS // SL) as j:
                for s in range(SL):
                    turn = SL * j + s
                    if s < SL - 1:
                        variances(turn + 1, s + 1, j)
                    else:
                        more = TURNS // SL - 1 - j
                        with dve.If(more):
                            variances(turn + 1, 0, j + 1)
                    for k in range(TT):
                        dve.wait_ge(n_done, turn * TT + k + 1)
                        dve.tensor_tensor(O[:, s, k], O[:, s, k], lng[:], ALU.mult).then_inc(g_done, 1)

        @block.gpsimd
        def _(pool):
            pool.wait_ge(ln_in, 32)
            with pool.Fori(0, TURNS // SL) as j:
                for s in range(SL):
                    for k in range(TT):
                        pool.wait_ge(g_done, (SL * j + s) * TT + k + 1)
                        pool.tensor_tensor(O[:, s, k], O[:, s, k], lnb[:], ALU.add).then_inc(o_done, 1)


class Kept:
    pass


def hybrid_layer(nc, x, w_in, b_in, conv_w, mh_g, w_out, ln_mix_g, ln_mix_b, router_w, router_b,
                 w_gate, w_up, w_down, ln_moe_g, ln_moe_b, out, alpha, n_groups):
    S, D = x.shape
    NE = router_w.shape[1]
    most = (2 * S + NE * (P - 1)) // P
    x1_dram = nc.dram_tensor("x1", [S, D], F32, kind="Internal").ap()
    acc_dram = nc.dram_tensor("gathered", [S + P, D], F32, kind="Internal").ap()
    ctx = ExitStack()
    with ctx:
        sb, ps, sem = tensors(nc, ctx, "kept")
        keep = Kept()
        keep.ident = sb("identity", [P, P])
        keep.conv_or_residual = sb("conv_or_residual", [P, 4 * (2 * BANK + 2)])
        keep.ln_bias = sb("ln_bias", [P, D])
        keep.first_in = sem("first_weights_in")
        mixer(nc, keep, x, w_in, b_in, conv_w, mh_g, w_out, ln_mix_g, ln_mix_b, x1_dram, acc_dram, alpha)
        keep.gather = sb("slot_gather_row", [P, most + 2], I32)
        keep.scatter = sb("slot_scatter_row", [P, most + 2], I32)
        keep.gate = sb("slot_gate", [P, most + 2])
        keep.table = sb("block_table", [1, 6, most + 2], I32)
        keep.raw = sb("w_raw", [P, (D + w_gate.shape[2]) // (2 * P), 2, D])
        route(nc, keep, x1_dram, acc_dram, router_w, router_b, w_gate, w_up, w_down, n_groups, alpha)
        experts(nc, keep, x1_dram, acc_dram, w_gate, w_up, w_down)
        final_norm(nc, acc_dram, ln_moe_g, ln_moe_b, out)


_STACKED = ("w_in", "b_in", "conv_w", "mh_norm_g", "w_out", "ln_mix_g", "ln_mix_b")
_SHARED = ("router_w", "router_b")
_EXPERT = ("w_gate", "w_up", "w_down", "ln_moe_g", "ln_moe_b")
N_EXPERT_GROUPS = 4


def kernel(**inputs):
    import numpy as _np
    import concourse.bacc as _bacc
    from concourse import mybir as _mybir
    from concourse.bass_utils import run_bass_kernel_spmd as _run

    nc = _bacc.Bacc("TRN2", target_bir_lowering=False, num_devices=1)
    x = _np.asarray(inputs["x"])
    depth = inputs["w_in"].shape[0]
    assert x.shape[0] == 1 and depth == 1
    arrays, args = {}, []
    for name in ("x",) + _STACKED + _SHARED + _EXPERT:
        a = _np.asarray(inputs[name])
        if name not in _SHARED:
            a = a[0]
        a = _np.ascontiguousarray(a)
        arrays[f"in_{name}"] = a
        args.append(nc.dram_tensor(f"in_{name}", a.shape, _mybir.dt.from_np(a.dtype), kind="ExternalInput").ap())
    out = nc.dram_tensor("out_x", x.shape[1:], _mybir.dt.from_np(x.dtype), kind="ExternalOutput").ap()
    hybrid_layer(nc, *args, out, alpha=(2 * depth) ** 0.25, n_groups=N_EXPERT_GROUPS)
    r = _run(nc, [arrays], core_ids=[0])
    return _np.asarray(r.results[0]["out_x"]).reshape(x.shape)
```
